# Optimizing a Trainium2 kernel written in Bass

```python
import jax, jax.numpy as jnp
from jax import lax
import numpy as np

D_MODEL = 1024
BATCH = 1
SEQ = 512
DEPTH = 1
DEC_BATCH = 8
DEC_SEQ = 1
PAST_LEN = 4096
PAGE_SIZE = 128

CHUNK_A = 128
A_WIDTH = D_MODEL
A_HEADS = 8
A_HEAD_DIM = A_WIDTH // A_HEADS
B_HEADS = 4
B_KEY_DIM = D_MODEL // 2
B_VAL_DIM = D_MODEL
B_HK = B_KEY_DIM // B_HEADS
B_HV = B_VAL_DIM // B_HEADS
GATE_RANK = 16
GATE_NORMALIZER = 16.0
CHUNK_B = 64
N_MEM = 256
C_HEADS = 4
C_WIDTH = D_MODEL
C_HD = C_WIDTH // C_HEADS
N_BRANCH = 3
EPS = 1e-6
IN_SIZES = (A_WIDTH, A_WIDTH, A_WIDTH, B_KEY_DIM, B_KEY_DIM, B_VAL_DIM, GATE_RANK,
            B_VAL_DIM, C_WIDTH, C_WIDTH, N_BRANCH * D_MODEL)
IN_COLS = sum(IN_SIZES)

kernel_name = "gated_parallel_gmlp_gla_memxattn_step"

def rmsnorm(x, g):
    xf = x.astype(jnp.float32)
    y = xf * lax.rsqrt(jnp.mean(xf * xf, axis=-1, keepdims=True) + EPS)
    return (y * g.astype(jnp.float32)).astype(x.dtype)

def layernorm(x, g, b):
    xf = x.astype(jnp.float32)
    mu = jnp.mean(xf, axis=-1, keepdims=True)
    var = jnp.mean(jnp.square(xf - mu), axis=-1, keepdims=True)
    y = (xf - mu) * lax.rsqrt(var + EPS)
    return (y * g.astype(jnp.float32) + b.astype(jnp.float32)).astype(x.dtype)

def split_proj(h, w_in):
    offs = np.cumsum(IN_SIZES)[:-1].tolist()
    return jnp.split(h @ w_in, offs, axis=-1)

def spatial_mix(vn, w_s, b_s, n_pos):
    wm = jnp.tril(w_s[:, :n_pos, :n_pos])
    s = jnp.einsum('hts,bnshc->bnthc', wm, vn)
    return s + b_s[:, :n_pos].T[:, :, None].astype(s.dtype)

def gla_prep(b_q, b_k, b_v, b_gd, w_g_up, b_g):
    lead = b_q.shape[:-1]
    f32 = jnp.float32
    q = b_q.astype(f32).reshape(*lead, B_HEADS, B_HK) * (B_HK ** -0.5)
    k = b_k.astype(f32).reshape(*lead, B_HEADS, B_HK)
    v = b_v.astype(f32).reshape(*lead, B_HEADS, B_HV)
    glog = jax.nn.log_sigmoid((b_gd @ w_g_up + b_g).astype(f32)) / GATE_NORMALIZER
    return q, k, v, glog.reshape(*lead, B_HEADS, B_HK)

def gla_chunked(q, k, v, g):
    Bn, T, H, K = q.shape
    V = v.shape[-1]
    n = T // CHUNK_B
    rs = lambda a: a.reshape(Bn, n, CHUNK_B, H, a.shape[-1])
    q, k, v, g = rs(q), rs(k), rs(v), rs(g)
    bcum = jnp.cumsum(g, axis=2)
    q_dec = q * jnp.exp(bcum)
    k_dec = k * jnp.exp(-bcum)
    mask = jnp.tril(jnp.ones((CHUNK_B, CHUNK_B), dtype=bool))
    scores = jnp.where(mask, jnp.einsum('bnchk,bnjhk->bnhcj', q_dec, k_dec), 0.0)
    o_intra = jnp.einsum('bnhcj,bnjhv->bnchv', scores, v)
    b_last = bcum[:, :, -1]
    chunk_kv = jnp.einsum('bnchk,bnchv->bnhkv', k * jnp.exp(b_last[:, :, None] - bcum), v)

    def step(S, xs):
        qd, bl, kv = xs
        o_inter = jnp.einsum('bchk,bhkv->bchv', qd, S)
        return jnp.exp(bl)[..., None] * S + kv, o_inter

    S0 = jnp.zeros((Bn, H, K, V), jnp.float32)
    S_fin, o_inter = lax.scan(step, S0, (jnp.moveaxis(q_dec, 1, 0), jnp.moveaxis(b_last, 1, 0),
                                         jnp.moveaxis(chunk_kv, 1, 0)))
    o = o_intra + jnp.moveaxis(o_inter, 0, 1)
    return o.reshape(Bn, T, H, V), S_fin

def gla_recurrent(q, k, v, g, S0):
    def step(S, xs):
        qt, kt, vt, gt = xs
        S = jnp.exp(gt)[..., None] * S + kt[..., None] * vt[..., None, :]
        return S, jnp.einsum('bhk,bhkv->bhv', qt, S)
    S, o = lax.scan(step, S0.astype(jnp.float32),
                    (jnp.moveaxis(q, 1, 0), jnp.moveaxis(k, 1, 0), jnp.moveaxis(v, 1, 0), jnp.moveaxis(g, 1, 0)))
    return jnp.moveaxis(o, 0, 1), S

def gla_out(o, gn_g, b_z, dtype):
    lead = o.shape[:-2]
    on = rmsnorm(o, gn_g).reshape(*lead, B_VAL_DIM).astype(dtype)
    return on * jax.nn.silu(b_z)

def mem_kv(mem, g_mem, w_mem_kv):
    kv = rmsnorm(mem, g_mem) @ w_mem_kv
    mk, mv = jnp.split(kv, 2, axis=-1)
    Bn = mem.shape[0]
    return mk.reshape(Bn, N_MEM, C_HEADS, C_HD), mv.reshape(Bn, N_MEM, C_HEADS, C_HD)

def cross_attn(c_q, mk, mv):
    lead = c_q.shape[:-1]
    q = c_q.reshape(*lead, C_HEADS, C_HD)
    s = jnp.einsum('bthd,bmhd->bhtm', q, mk).astype(jnp.float32) * (C_HD ** -0.5)
    p = jax.nn.softmax(s, axis=-1).astype(mv.dtype)
    return jnp.einsum('bhtm,bmhd->bthd', p, mv).reshape(*lead, C_WIDTH)

def merge(gate_logits, b_gate, outs, w_branch, w_out):
    lead = gate_logits.shape[:-1]
    gates = jax.nn.sigmoid(gate_logits + b_gate).reshape(*lead, N_BRANCH, D_MODEL)
    br = jnp.stack(outs, axis=-2)
    proj = jnp.einsum('btic,icd->btid', br, w_branch)
    return jnp.sum(gates * proj, axis=-2) @ w_out

def layer_prompt(x, mem, l, p):
    (g_norm, w_in, b_gate, w_s, b_s, ln_v_g, ln_v_b, w_g_up, b_g, gn_g,
     g_mem, w_mem_kv, w_branch, w_out) = p
    Bn, T, _ = x.shape
    h = rmsnorm(x, g_norm[l])
    a_u, a_v, a_z, b_q, b_k, b_v, b_gd, b_z, c_q, c_z, gl = split_proj(h, w_in[l])
    a_u, a_v = jax.nn.gelu(a_u), jax.nn.gelu(a_v)
    vn = layernorm(a_v, ln_v_g[l], ln_v_b[l]).reshape(Bn, T // CHUNK_A, CHUNK_A, A_HEADS, A_HEAD_DIM)
    s = spatial_mix(vn, w_s[l], b_s[l], CHUNK_A).reshape(Bn, T, A_WIDTH)
    out_a = a_u * s * jax.nn.silu(a_z)
    q, k, v, g = gla_prep(b_q, b_k, b_v, b_gd, w_g_up[l], b_g[l])
    o, S = gla_chunked(q, k, v, g)
    out_b = gla_out(o, gn_g[l], b_z, x.dtype)
    mk, mv = mem_kv(mem, g_mem[l], w_mem_kv[l])
    out_c = cross_attn(c_q, mk, mv) * jax.nn.silu(c_z)
    x = x + merge(gl, b_gate[l], (out_a, out_b, out_c), w_branch[l], w_out[l])
    return x, S, mk, mv

def layer_sample(x, S0, mk, mv, l, p):
    (g_norm, w_in, b_gate, w_s, b_s, ln_v_g, ln_v_b, w_g_up, b_g, gn_g,
     g_mem, w_mem_kv, w_branch, w_out) = p
    Bn, T, _ = x.shape
    h = rmsnorm(x, g_norm[l])
    a_u, a_v, a_z, b_q, b_k, b_v, b_gd, b_z, c_q, c_z, gl = split_proj(h, w_in[l])
    a_u, a_v = jax.nn.gelu(a_u), jax.nn.gelu(a_v)
    vn = layernorm(a_v, ln_v_g[l], ln_v_b[l]).reshape(Bn, T, A_HEADS, A_HEAD_DIM)
    s = spatial_mix(vn[:, None], w_s[l], b_s[l], T)[:, 0].reshape(Bn, T, A_WIDTH)
    out_a = a_u * s * jax.nn.silu(a_z)
    q, k, v, g = gla_prep(b_q, b_k, b_v, b_gd, w_g_up[l], b_g[l])
    o, S = gla_recurrent(q, k, v, g, S0)
    out_b = gla_out(o, gn_g[l], b_z, x.dtype)
    out_c = cross_attn(c_q, mk, mv) * jax.nn.silu(c_z)
    x = x + merge(gl, b_gate[l], (out_a, out_b, out_c), w_branch[l], w_out[l])
    return x, S, vn

def setup_inputs(seed: int = 0) -> dict:
    key = jax.random.key(seed)
    ks = jax.random.split(key, 24)
    f32 = jnp.float32
    nrm = lambda k, shape, sc: jax.random.normal(k, shape, f32) * sc
    return {
        "x_prompt": nrm(ks[0], (BATCH, SEQ, D_MODEL), 1.0),
        "x_sample": nrm(ks[1], (DEC_BATCH, DEC_SEQ, D_MODEL), 1.0),
        "state_gla": nrm(ks[2], (DEPTH, DEC_BATCH, B_HEADS, B_HK, B_HV), 0.5),
        "cache_mem_k": nrm(ks[3], (DEPTH, DEC_BATCH, N_MEM, C_HEADS, C_HD), 1.0),
        "cache_mem_v": nrm(ks[4], (DEPTH, DEC_BATCH, N_MEM, C_HEADS, C_HD), 1.0),
        "mem_prompt": nrm(ks[5], (BATCH, N_MEM, D_MODEL), 1.0),
        "g_norm": 1.0 + nrm(ks[6], (DEPTH, D_MODEL), 0.05),
        "w_in": nrm(ks[7], (DEPTH, D_MODEL, IN_COLS), D_MODEL ** -0.5),
        "b_gate": nrm(ks[8], (DEPTH, N_BRANCH * D_MODEL), 0.1),
        "w_s": nrm(ks[9], (DEPTH, A_HEADS, CHUNK_A, CHUNK_A), CHUNK_A ** -0.5),
        "b_s": 1.0 + nrm(ks[10], (DEPTH, A_HEADS, CHUNK_A), 0.1),
        "ln_v_g": 1.0 + nrm(ks[11], (DEPTH, A_WIDTH), 0.05),
        "ln_v_b": nrm(ks[12], (DEPTH, A_WIDTH), 0.05),
        "w_g_up": nrm(ks[13], (DEPTH, GATE_RANK, B_KEY_DIM), GATE_RANK ** -0.5),
        "b_g": nrm(ks[14], (DEPTH, B_KEY_DIM), 0.1),
        "gn_g": 1.0 + nrm(ks[15], (DEPTH, B_HV), 0.05),
        "g_mem": 1.0 + nrm(ks[16], (DEPTH, D_MODEL), 0.05),
        "w_mem_kv": nrm(ks[17], (DEPTH, D_MODEL, 2 * C_WIDTH), D_MODEL ** -0.5),
        "w_branch": nrm(ks[18], (DEPTH, N_BRANCH, A_WIDTH, D_MODEL), A_WIDTH ** -0.5),
        "w_out": nrm(ks[19], (DEPTH, D_MODEL, D_MODEL), D_MODEL ** -0.5),
        "g_final": 1.0 + nrm(ks[20], (D_MODEL,), 0.05),
    }

def reference(x_prompt, x_sample, state_gla, cache_mem_k, cache_mem_v, mem_prompt,
              g_norm, w_in, b_gate, w_s, b_s, ln_v_g, ln_v_b, w_g_up, b_g, gn_g,
              g_mem, w_mem_kv, w_branch, w_out, g_final):
    p = (g_norm, w_in, b_gate, w_s, b_s, ln_v_g, ln_v_b, w_g_up, b_g, gn_g,
         g_mem, w_mem_kv, w_branch, w_out)
    xp, xs = x_prompt, x_sample
    gla_p, mk_p, mv_p, gla_s, v_s = [], [], [], [], []
    for l in range(DEPTH):
        xp, S_p, mk, mv = layer_prompt(xp, mem_prompt, l, p)
        gla_p.append(S_p)
        mk_p.append(mk)
        mv_p.append(mv)
        xs, S_s, vn = layer_sample(xs, state_gla[l], cache_mem_k[l], cache_mem_v[l], l, p)
        gla_s.append(S_s)
        v_s.append(vn)
    y_prompt = rmsnorm(xp, g_final)
    y_sample = rmsnorm(xs, g_final)
    state_gla_prompt = jnp.stack(gla_p).astype(x_prompt.dtype)
    cache_mem_k_prompt = jnp.stack(mk_p)
    cache_mem_v_prompt = jnp.stack(mv_p)
    state_gla_sample = jnp.stack(gla_s).astype(x_sample.dtype)
    state_gmlp_v_sample = jnp.stack(v_s)
    return (y_prompt, y_sample, state_gla_prompt, cache_mem_k_prompt, cache_mem_v_prompt,
            state_gla_sample, state_gmlp_v_sample)


_drawn_inputs = setup_inputs


def setup_inputs(seed=0):
    import zlib

    import numpy as np

    out = dict(_drawn_inputs(seed))
    spreads = {}
    factors = {'b_gate': 3.911, 'b_s': 2.957, 'gn_g': 4.042, 'cache_mem_k': 3.839, 'cache_mem_v': 3.033}
    for name, (base, spread) in spreads.items():
        noise = np.random.default_rng([zlib.crc32(name.encode()), seed]).standard_normal(out[name].shape)
        drawn = base * np.exp(spread * noise) if base else spread * noise
        out[name] = __import__('jax').numpy.asarray(drawn.astype(out[name].dtype))
    for name, factor in factors.items():
        out[name] = (out[name] * factor).astype(out[name].dtype)
    return out
```

```python
from contextlib import ExitStack

import concourse.bass as bass
from concourse import mybir

ALU = mybir.AluOpType
ACT = mybir.ActivationFunctionType
F32 = mybir.dt.float32
F32R = mybir.dt.float32r
AX_X = mybir.AxisListType.X

P = 128
D = 1024
KT = D // P
T = 512
NT = T // P
B = 8
TT = T + B
HALF = TT // 2
MEM = 256
MT = MEM // P
BH, BK, BV = 4, 128, 256
CH = 4
CD = 256
AH = 8
RANK = 16
SUB = 64
EPS = 1e-6
Q_SCALE = BK ** -0.5
C_SCALE = CD ** -0.5
TRI = 1.0 / 16.0

O_AU, O_AV, O_AZ = 0, D, 2 * D
O_QK = 3 * D
O_BV = O_QK + D
O_GD = O_BV + D
O_BZ = O_GD + RANK
O_CQ = O_BZ + D
O_CZ = O_CQ + D
O_GA = O_CZ + D
O_GB = O_GA + D
O_GC = O_GB + D

NAMES = ["K", "V", "QK", "BV", "BZ", "CQ", "GB", "AZ", "PB", "AV", "AU", "GA", "PA", "CZ", "GC", "PC", "OUT"]
BLK = {n: i for i, n in enumerate(NAMES)}
NTILES = KT * len(NAMES)
TR = {n: KT * i for i, n in enumerate(["K", "V", "BV", "AV", "OUT"])}
ST = {n: KT * i for i, n in enumerate(["PB", "AU", "PA", "PC"])}
IRREGULAR = {"K", "BZ", "CQ", "GB", "AZ", "PB", "AV", "AU", "GA", "PA", "CZ", "GC", "OUT"}


def first(name):
    return KT * BLK[name]


def wait(eng, sem, value):
    if isinstance(value, int) and value <= 0:
        return
    eng.wait_ge(sem, value)


def over_block(eng, name, body):
    if name in IRREGULAR:
        for it in range(2):
            body(it, first(name) + 4 * it)
    else:
        with eng.Fori(0, 2) as it:
            body(it, it * 4 + first(name))


def bass_gated_parallel_step(nc, x_prompt, x_sample, state_gla, cache_mem_k, cache_mem_v,
                             mem_prompt, g_norm, w_in, b_gate, w_s, b_s, ln_v_g, ln_v_b, w_g_up,
                             b_g, gn_g, g_mem, w_mem_kv, w_branch, w_out, g_final,
                             y_prompt, y_sample, st_prompt, k_prompt, v_prompt, st_sample,
                             vn_sample):
    scr_kT = nc.dram_tensor("scr_kT", [P, KT, MEM], F32, kind="Internal").ap()
    scr_qT = nc.dram_tensor("scr_qT", [P, KT, T], F32, kind="Internal").ap()
    scr_v = nc.dram_tensor("scr_v", [B, D], F32, kind="Internal").ap()
    scr_q = nc.dram_tensor("scr_q", [B, D], F32, kind="Internal").ap()

    win = w_in[0]
    source = {
        "K": w_mem_kv[0][:, 0:D], "V": w_mem_kv[0][:, D:2 * D],
        "QK": win[:, O_QK:O_QK + D], "BV": win[:, O_BV:O_BV + D], "BZ": win[:, O_BZ:O_BZ + D],
        "CQ": win[:, O_CQ:O_CQ + D], "GB": win[:, O_GB:O_GB + D], "AZ": win[:, O_AZ:O_AZ + D],
        "PB": w_branch[0, 1], "AV": win[:, O_AV:O_AV + D], "AU": win[:, O_AU:O_AU + D],
        "GA": win[:, O_GA:O_GA + D], "PA": w_branch[0, 0], "CZ": win[:, O_CZ:O_CZ + D],
        "GC": win[:, O_GC:O_GC + D], "PC": w_branch[0, 2], "OUT": w_out[0],
    }

    with ExitStack() as ctx:
        def sb(name, shape, dt=F32):
            return ctx.enter_context(nc.sbuf_tensor(name, shape, dt))

        def overlay(*layouts):
            out = []
            for n, layout in enumerate(layouts):
                own = ExitStack()
                out.append([own.enter_context(nc.sbuf_tensor(*t)) for t in layout])
                if n < len(layouts) - 1:
                    own.close()
                else:
                    ctx.enter_context(own)
            return out

        sems = {}

        def sem(name):
            if name not in sems:
                sems[name] = ctx.enter_context(nc.semaphore(name))
            return sems[name]

        h_hi = sb("h_hi", [P, KT, TT], F32R)
        h_lo = sb("h_lo", [P, KT, TT], F32R)
        x_hi = sb("x_hi", [P, KT, TT], F32R)
        x_lo = sb("x_lo", [P, KT, TT], F32R)
        gate = sb("gate", [P, KT, TT])
        mz = sb("mz", [P, KT, TT])
        t1 = sb("t1", [P, KT, TT])
        raw = sb("raw", [P, 2, KT, 2 * P])
        w_hi = sb("w_hi", [P, 4, KT, P], F32R)
        w_lo = sb("w_lo", [P, 4, KT, P], F32R)
        stage = sb("stage", [P, 2, TT])
        (att, (tok,)) = overlay(
            [("k_hi", [P, 2, MEM], F32R), ("k_lo", [P, 2, MEM], F32R),
             ("v_hi", [P, MT, CD], F32R), ("v_lo", [P, MT, CD], F32R),
             ("pT_hi", [P, MT, T], F32R), ("pT_lo", [P, MT, T], F32R)],
            [("tok", [P, NT, D], F32)])
        k_hi, k_lo, v_hi, v_lo, pT_hi, pT_lo = att
        ((gd_hi, gd_lo, gd_raw), (work,)) = overlay(
            [("gd_hi", [P, KT, P], F32R), ("gd_lo", [P, KT, P], F32R), ("gd_raw", [P, KT, P], F32)],
            [("work", [P, 3840], F32)])
        state = sb("state", [P, BH, BV])
        stok = sb("stok", [B, D])
        ident = sb("ident", [P, P])
        tri = sb("tri", [P, 2, P])
        gn1 = sb("gn1", [P, KT])
        gm1 = sb("gm1", [P, KT])
        bg1 = sb("bg1", [P, 3 * KT])
        gnc = sb("gnc", [P, 2])
        small = sb("small", [P, 96])
        qsT = sb("qsT", [P, KT, B])
        hs = sb("hs", [P, KT, B])
        ksT = sb("ksT", [P, BH, B])
        ocs = sb("ocs", [P, KT, B])
        w00 = sb("w00", [P, AH])
        ssq, rstd = small[:, 0:8], small[:, 8:16]
        cols = small[:, 16:24].rearrange("p (h c) -> p h c", c=2)
        e_last = small[:, 24:28]
        mx, nmx, den, rden = small[:, 28:32], small[:, 32:36], small[:, 36:40], small[:, 40:44]
        stats = small[:, 44:56].rearrange("p (a c) -> p a c", c=6)
        mv = small[:, 56:58]
        lstd = small[:, 58:59]
        lrst = small[:, 59:60]
        kss_last = small[:, 60:64]
        dstat = small[:, 64:70]
        eps_col = small[:, 70:71]

        def piece(base, at, shape):
            n = 1
            for s in shape:
                n *= s
            v = base[:, at:at + n]
            if len(shape) == 2:
                v = v.rearrange("p (a b) -> p a b", b=shape[1])
            if len(shape) == 3:
                v = v.rearrange("p (a b c) -> p a b c", b=shape[1], c=shape[2])
            return v

        eb = piece(work, 0, (BH, P))
        enb = piece(work, 512, (BH, P))
        eB = piece(work, 1024, (BH, P))
        eBl = piece(work, 1536, (BH, P))
        e5 = piece(work, 2048, (BH, SUB))
        gl = piece(work, 2304, (512,))
        ktk = piece(work, 2816, (BH, P))
        ssb = piece(work, 3328, (BH, P))
        on = piece(work, 0, (D,))
        tok_flat = tok[:, :, :].rearrange("p n d -> p (n d)")
        s_in = piece(tok_flat, 0, (2, BH, BV))
        v_bc = piece(tok_flat, 2048, (2, D))
        egs = piece(work, 0, (BH, B))
        zs = piece(work, 32, (BH, B))
        qmask = piece(work, 64, (BH, B, B))
        ons = piece(work, 512, (BV,))
        tmp_kv = piece(work, 1536, (BH, BV))
        zmn = piece(work, 2560, (BH, B))
        lng = piece(work, 0, (D,))
        lnb = piece(work, D, (D,))
        bs_bc = piece(work, 2 * D, (AH, P))
        mtmp = piece(work, 3 * D, (TT,))
        wsT = state[:, :, :].rearrange("p h v -> p (h v)").rearrange("p (h t) -> p h t", t=P)
        gate_flat = gate[:, :, :].rearrange("p k t -> p (k t)")
        mz_flat = mz[:, :, :].rearrange("p k t -> p (k t)")
        t1_flat = t1[:, :, :].rearrange("p k t -> p (k t)")
        ws_raw = piece(gate_flat, 0, (AH, P))
        w_up = gate[0:RANK + 1, 6, 0:512]
        gdT = gate[0:RANK + 1, 7, :]
        mem_in = piece(gate_flat, 0, (MT, D))
        xs_in = mz_flat[0:B, 0:D]
        junk = mz_flat[:, D:2 * D]
        x_in = piece(t1_flat, 0, (NT, D))
        kc = piece(gate_flat, 0, (2, D))
        q_bc = piece(gate_flat, 2 * D, (2, D))
        p32 = gate_flat[0:B * CH, 2 * D:2 * D + MEM]
        pz = piece(work, 3592, (MT, B, 2 * CH))
        sc = piece(work, 3744, (MT, B * CH))
        sel = piece(work, 3808, (CH, 2, 4))
        o_sb = piece(work, 2 * D, (D,))
        v_slots = [work[:, 0:D], work[:, D:2 * D]] + [tok[:, (i - 2) % 4, :] for i in range(2, B * MT)]
        q_raw = piece(work, 0, (2, T))
        k_raw = piece(work, 1024, (2, MEM))
        v_raw = piece(work, 1536, (MT, CD))
        prob = piece(work, 2048, (NT, MEM))
        gf_bc = piece(work, 0, (D,))
        junk2 = piece(work, D, (D,))

        mm = ctx.enter_context(nc.psum_tensor("mm", [P, 2, 2, 512], F32))
        p45 = ctx.enter_context(nc.psum_tensor("p45", [P, 2, 512], F32))
        p67 = ctx.enter_context(nc.psum_tensor("p67", [P, 2, 512], F32))
        p45_8 = p45[:, :, :].rearrange("p a (b c) -> p (a b) c", c=P)
        p67_8 = p67[:, :, :].rearrange("p a (b c) -> p (a b) c", c=P)
        p45_4 = p45[:, :, :].rearrange("p a (b c) -> p (a b) c", c=256)
        p67_4 = p67[:, :, :].rearrange("p a (b c) -> p (a b) c", c=256)

        w_loaded = [sem("w_loaded0"), sem("w_loaded1")]
        hi_ready = sem("hi_ready")
        split_done = sem("split_done")
        prod_done = sem("prod_done")
        evac_done = sem("evac_done")
        tr_done = sem("tr_done")
        tr_used = sem("tr_used")
        stage_used = sem("stage_used")
        spilled = {n: [sem(f"{n}_spilled0"), sem(f"{n}_spilled1")] for n in ("K", "CQ")}

        block = ctx.enter_context(nc.Block())

        @block.sync
        def _(sp):
            sp.dma_start(mem_in, mem_prompt[0].rearrange("(n p) d -> p n d", p=P)).then_inc(sem("mem_loaded"), 16)
            sp.dma_start(raw[:, 0], source["K"][:, 0:256].rearrange("(k p) c -> p k c", p=P)).then_inc(w_loaded[0], 16)
            sp.dma_start(x_in, x_prompt[0].rearrange("(n p) d -> p n d", p=P)).then_inc(sem("x_loaded"), 16)
            for name in NAMES:
                def body(it, g):
                    for s in range(2):
                        if name == "K" and isinstance(it, int) and it == 0 and s == 0:
                            continue
                        wait(sp, split_done, g + 2 * s - 2)
                        src = source[name][:, bass.ds(it * 512 + 256 * s, 256)]
                        sp.dma_start(raw[:, s], src.rearrange("(k p) c -> p k c", p=P)).then_inc(w_loaded[s], 16)
                if name == "K":
                    for it in range(2):
                        body(it, 4 * it)
                else:
                    with sp.Fori(0, 2) as it:
                        body(it, it * 4 + first(name))

        @block.gpsimd
        def _(pool):
            steps = [0]

            def link(*instructions):
                for ins in instructions:
                    ins.then_inc(sem("pool_link"), 1)
                steps[0] += len(instructions)
                pool.wait_ge(sem("pool_link"), steps[0])

            with nc.allow_non_contiguous_dma(reason="parameters by channel, a few KB"):
                pool.dma_start(gm1[:, :], g_mem[0].rearrange("(k p) -> p k", p=P)).then_inc(sem("start_loaded"), 16)
                pool.dma_start(xs_in, x_sample.rearrange("b t d -> (b t) d")).then_inc(sem("start_loaded"), 16)
                pool.dma_start(gn1[:, :], g_norm[0].rearrange("(k p) -> p k", p=P)).then_inc(sem("start_loaded"), 16)
            link(pool.memset(ident[:, :], 0.0), pool.memset(tri[:, :, :], TRI))
            pool.affine_select(out=ident[:, :], in_=ident[:, :], compare_op=ALU.not_equal, fill=1.0, base=0,
                               pattern=[[-1, P]], channel_multiplier=1).then_inc(sem("ident_ready"), 1)
            link(*[pool.affine_select(out=tri[:, a, :], in_=tri[:, a, :], compare_op=ALU.is_ge, fill=0.0, base=0,
                                      pattern=[[1, P]], channel_multiplier=-1) for a in range(2)])
            pool.memset(tri[0:SUB, 0, SUB:P], 0.0).then_inc(sem("tri_ready"), 1)
            with nc.allow_non_contiguous_dma(reason="parameters by channel, a few KB"):
                pool.dma_start(bg1[:, :], b_gate[0].rearrange("(k p) -> p k", p=P)).then_inc(sem("params_loaded"), 16)
                pool.dma_start(gnc[:, :], gn_g[0].rearrange("(k p) -> p k", p=P)).then_inc(sem("params_loaded"), 16)
                pool.dma_start(w00[:, :], w_s[0, :, 0, 0:1].rearrange("h o -> o h").broadcast_to([P, AH])).then_inc(sem("params_loaded"), 16)
                pool.dma_start(gd_raw[:, :, :], win[:, O_GD:O_GD + P].rearrange("(k p) c -> p k c", p=P)).then_inc(sem("params_loaded"), 16)
            pool.wait_ge(sem("memT_done"), KT)
            pool.dma_start(gate[0:RANK, 6, 0:512], w_g_up[0]).then_inc(sem("up_loaded"), 16)
            pool.dma_start(gate[RANK:RANK + 1, 6, 0:512], b_g[0:1, :]).then_inc(sem("up_loaded"), 16)

            for j in range(KT):
                pool.wait_ge(evac_done, j + 1)
                pool.dma_start(scr_kT[:, j, :], stage[:, j % 2, 0:MEM]).then_inc(spilled["K"][j % 2], 16)
            pool.wait_ge(tr_used, KT)
            pool.dma_start(k_prompt[0, 0].rearrange("(n p) h d -> p n (h d)", p=P), tok[:, 0:2, :]).then_inc(sem("kv_stored"), 16)
            pool.wait_ge(tr_used, 2 * KT)
            pool.dma_start(v_prompt[0, 0].rearrange("(n p) h d -> p n (h d)", p=P), tok[:, 2:4, :]).then_inc(sem("kv_stored"), 16)
            pool.wait_ge(tr_used, TR["BV"] + KT)
            pool.dma_start(scr_v, stok[:, :]).then_inc(sem("vs_stored"), 16)
            for j in range(KT):
                pool.wait_ge(evac_done, first("CQ") + j + 1)
                pool.dma_start(scr_qT[:, j, :], stage[:, j % 2, 0:T]).then_inc(spilled["CQ"][j % 2], 16)
            pool.wait_ge(sem("vs_stored"), 16)
            pool.wait_ge(sem("o_done"), NT)
            pool.wait_ge(sem("kv_done"), NT)
            for b in range(B):
                s = b % 2
                if b >= 2:
                    pool.wait_ge(sem(f"ss_stored{s}"), 16 * (b // 2))
                    pool.wait_ge(sem("so_done"), b - 1)
                pool.dma_start(s_in[:, s], state_gla[0, b].rearrange("h k v -> k h v")).then_inc(sem(f"ss_loaded{s}"), 16)
                pool.dma_start(v_bc[:, s], scr_v[b:b + 1, :].broadcast_to([P, D])).then_inc(sem(f"ss_loaded{s}"), 16)
                if b >= 1:
                    pool.wait_ge(sem("ss_ready"), BH * b)
                    pool.dma_start(st_sample[0, b - 1].rearrange("h k v -> k h v"), s_in[:, 1 - s]).then_inc(sem(f"ss_stored{1 - s}"), 16)
            pool.wait_ge(sem("ss_ready"), BH * B)
            pool.dma_start(st_sample[0, B - 1].rearrange("h k v -> k h v"), s_in[:, 1]).then_inc(sem("ss_stored1"), 16)
            pool.wait_ge(sem("state_ready"), NT)
            pool.dma_start(st_prompt[0, 0].rearrange("h k v -> k h v"), state[:, :, :]).then_inc(sem("st_stored"), 16)
            pool.wait_ge(sem("dq_ready"), 1)
            pool.dma_start(scr_q, work[0:B, 2048:2048 + D]).then_inc(sem("dq_stored"), 16)
            pool.wait_ge(sem("dq_stored"), 16)
            pool.wait_ge(sem("obs_ready"), 1)
            pool.memset(pz.rearrange("p m b c -> p (m b c)"), 0.0).then_inc(sem("sel_ready"), 1)
            link(pool.memset(sel.rearrange("p h g j -> p (h g j)"), 0.0))
            pool.affine_select(out=sel, in_=sel, compare_op=ALU.not_equal, fill=1.0, base=0,
                               pattern=[[-1, CH], [-4, 2], [-32, 4]], channel_multiplier=1).then_inc(sem("sel_ready"), 1)
            pool.dma_start(lng, ln_v_g[0:1, :].broadcast_to([P, D])).then_inc(sem("a_loaded"), 16)
            pool.dma_start(lnb, ln_v_b[0:1, :].broadcast_to([P, D])).then_inc(sem("a_loaded"), 16)
            pool.dma_start(bs_bc.rearrange("p h t -> p (h t)"), b_s.rearrange("l h t -> l (h t)").broadcast_to([P, D])).then_inc(sem("a_loaded"), 16)
            pool.wait_ge(stage_used, ST["PB"] + KT)
            for i in range(B * MT):
                if i >= 2:
                    pool.wait_ge(sem("dsc_done"), CH * (i - 1))
                if i % 2 == 0:
                    pool.dma_start(q_bc[:, i // 2 % 2], scr_q[i // 2:i // 2 + 1, :].broadcast_to([P, D])).then_inc(sem(f"qb_loaded{i // 2 % 2}"), 16)
                src = cache_mem_k[0, i // 2].rearrange("(n p) h d -> p n (h d)", p=P)[:, i % 2, :]
                pool.dma_start(kc[:, i % 2], src).then_inc(sem(f"kc_loaded{i % 2}"), 16)
            pool.wait_ge(sem("dsc_done"), CH * B * MT)
            pool.dma_start(ws_raw, w_s[0].rearrange("h t s -> t h s")).then_inc(sem("ws_loaded"), 16)
            pool.wait_ge(sem("a_loaded"), 48)
            for n in range(NT):
                pool.wait_ge(sem("ln_norm"), n + 1)
                link(pool.tensor_tensor(tok[:, n, :], tok[:, n, :], lng, ALU.mult))
                pool.tensor_tensor(tok[:, n, :], tok[:, n, :], lnb, ALU.add).then_inc(sem("vn_ready"), 1)
            pool.wait_ge(sem("vns_ready"), 1)
            pool.dma_start(vn_sample.rearrange("l b t h c -> (l b t) (h c)"), stok[:, :]).then_inc(sem("vns_stored"), 16)

            def load_v(i):
                g, m, j = i // 8, i // 4 % 2, i % 4
                src = cache_mem_v[0, 4 * g + j].rearrange("(n p) h d -> p n (h d)", p=P)[:, m, :]
                slot = "w" if i < 2 else str((i - 2) % 4)
                pool.dma_start(v_slots[i], src).then_inc(sem("vc_loaded" + slot), 16)

            pool.wait_ge(sem("vn_ready"), NT)
            pool.wait_ge(sem("vns_ready"), 1)
            load_v(0)
            load_v(1)
            pool.wait_ge(sem("mix_done"), AH)
            for i in range(2, B * MT):
                if i >= 6:
                    pool.wait_ge(sem("dpv_done"), i - 3)
                load_v(i)

            pool.wait_ge(sem("mix_lo"), AH)
            for n in range(2):
                pool.wait_ge(spilled["K"][n], 16 * KT // 2)
                pool.wait_ge(spilled["CQ"][n], 16 * KT // 2)
            pool.wait_ge(sem("kv_stored"), 32)
            for h in range(CH):
                if h >= 1:
                    pool.wait_ge(sem("ap_lo"), 3 * h)
                pool.dma_start(q_raw, scr_qT[:, 2 * h:2 * h + 2, :]).then_inc(sem("att_loaded"), 16)
                pool.dma_start(k_raw, scr_kT[:, 2 * h:2 * h + 2, :]).then_inc(sem("att_loaded"), 16)
                pool.dma_start(v_raw, v_prompt[0, 0].rearrange("(n p) h d -> p n h d", p=P)[:, :, h, :]).then_inc(sem("att_loaded"), 16)

            pool.wait_ge(sem("oc_lo"), CH + 1)
            pool.dma_start(x_in, x_prompt[0].rearrange("(n p) d -> p n d", p=P)).then_inc(sem("end_loaded"), 16)
            pool.dma_start(gf_bc, g_final.rearrange("(a d) -> a d", a=1).broadcast_to([P, D])).then_inc(sem("end_loaded"), 16)
            pool.wait_ge(sem("merged"), 2 * KT)
            pool.wait_ge(sem("m_hi"), KT)
            pool.wait_ge(sem("m_lo"), KT)
            pool.dma_start(xs_in, x_sample.rearrange("b t d -> (b t) d")).then_inc(sem("end_loaded"), 16)
            for n in range(NT):
                pool.wait_ge(sem("y_ready"), n + 1)
                pool.dma_start(y_prompt[0, n * P:(n + 1) * P, :], tok[:, n, :]).then_inc(sem("y_stored"), 16)
            pool.wait_ge(sem("y_ready"), NT + 1)
            pool.dma_start(y_sample.rearrange("b t d -> (b t) d"), stok[:, :]).then_inc(sem("y_stored"), 16)
            pool.wait_ge(sem("kv_stored"), 32)
            pool.wait_ge(sem("kv_stored"), 32)
            pool.wait_ge(sem("ss_stored0"), 16 * B // 2)
            pool.wait_ge(sem("ss_stored1"), 16 * B // 2)
            pool.wait_ge(sem("st_stored"), 16)
            pool.wait_ge(sem("vns_stored"), 16)
            pool.wait_ge(sem("y_stored"), 16 * (NT + 1))

        @block.scalar
        def _(act):
            A = nc.scalar.activation
            steps = [0]

            def link(*instructions):
                for ins in instructions:
                    ins.then_inc(sem("act_link"), 1)
                steps[0] += len(instructions)
                act.wait_ge(sem("act_link"), steps[0])

            def hi(t, j, pair_loads):
                if isinstance(t, int) and t >= NTILES:
                    return
                act.wait_ge(w_loaded[j // 2], pair_loads)
                wait(act, prod_done, t - 3)
                A(w_hi[:, j], raw[:, j // 2, :, (j % 2) * P:(j % 2 + 1) * P], ACT.Copy).then_inc(hi_ready, 1)

            def square(rows, out, col):
                n = rows.shape[0]
                return A(out, rows, ACT.Square, accum_out=ssq[0:n, col:col + 1])

            act.wait_ge(sem("mem_loaded"), 16)
            act.wait_ge(sem("eps_ready"), 1)
            for n in range(MT):
                link(square(mem_in[:, n, :], junk, n))
            A(rstd[:, 0:MT], ssq[:, 0:MT], ACT.Sqrt, scale=1.0 / D, bias=eps_col[:, :]).then_inc(sem("rt_mem"), 1)
            hi(0, 0, 16)
            hi(1, 1, 16)
            act.wait_ge(sem("start_loaded"), 48)
            for k in range(KT):
                act.wait_ge(sem("memT_done"), k + 1)
                A(x_hi[:, k, 0:MEM], p45[:, k % 2, 0:MEM], ACT.Copy, scale=gm1[:, k:k + 1]).then_inc(sem("memT_hi"), 1)

            def x_norm():
                act.wait_ge(sem("x_loaded"), 16)
                act.wait_ge(sem("start_loaded"), 48)
                act.wait_ge(sem("mem_n"), MT)
                for n in range(NT):
                    link(square(x_in[:, n, :], junk, n))
                link(square(xs_in, junk[0:B, :], NT))
                A(rstd[:, 0:NT], ssq[:, 0:NT], ACT.Sqrt, scale=1.0 / D, bias=eps_col[:, :]).then_inc(sem("rt_x"), 1)
                A(rstd[0:B, NT:NT + 1], ssq[0:B, NT:NT + 1], ACT.Sqrt, scale=1.0 / D, bias=eps_col[0:B, :]).then_inc(sem("rt_x"), 1)
                act.wait_ge(sem("start_loaded"), 48)

            def x_hi_part(k):
                act.wait_ge(sem("xT_done"), k + 1)
                A(h_hi[:, k, 0:T], p67[:, k % 2, :], ACT.Copy, scale=gn1[:, k:k + 1]).then_inc(sem("xT_hi"), 1)

            def evac(name, it, j, g):
                t = g + j
                c = it * 4 + j
                act.wait_ge(prod_done, t + 1)
                src = mm[:, j % 2, :, 0:HALF]
                if name in TR:
                    wait(act, tr_done, c + (TR[name] - 1))
                if name in ST:
                    wait(act, stage_used, c + (ST[name] - 1))
                at_start = isinstance(it, int) and it == 0 and j < 2
                if name == "K" and not at_start:
                    act.wait_ge(spilled["K"][j % 2], 16 * (c // 2))
                if name == "CQ":
                    if at_start:
                        act.wait_ge(tr_done, TR["BV"] + KT)
                    else:
                        act.wait_ge(spilled["CQ"][j % 2], 16 * (c // 2))

                def out3(buf):
                    return buf[:, bass.ds(c, 1), :].rearrange("p o (a b) -> p (o a) b", a=2)

                st = stage[:, j % 2, :].rearrange("p (a b) -> p a b", a=2)
                if name in ("K", "V"):
                    ins = A(stage[:, j % 2, 0:MEM], mm[:, j % 2, 0, 0:MEM], ACT.Copy)
                elif name in ("BV", "PB", "PA", "PC", "OUT"):
                    ins = A(st, src, ACT.Copy)
                elif name == "CQ":
                    A(qsT[:, c, :], mm[:, j % 2, 1, HALF - B:HALF], ACT.Copy).then_inc(sem("qs_ready"), 1)
                    ins = A(st, src, ACT.Copy)
                elif name == "QK":
                    ins = A(out3(t1), src, ACT.Copy)
                elif name == "BZ":
                    ins = A(out3(mz), src, ACT.Silu)
                elif name in ("AZ", "CZ"):
                    ins = A(out3(t1), src, ACT.Silu)
                elif name in ("AV", "AU"):
                    ins = A(st, src, ACT.Gelu_apprx_tanh)
                else:
                    i = "ABC".index(name[1])
                    ins = A(out3(gate), src, ACT.Sigmoid, bias=bg1[:, i * KT + c:i * KT + c + 1])
                ins.then_inc(evac_done, 1)

            def hooks(name, c):
                if name == "K":
                    if c == 0:
                        x_norm()
                    elif c <= 4:
                        x_hi_part(2 * c - 2)
                        x_hi_part(2 * c - 1)
                    elif c == 5:
                        act.wait_ge(sem("xsT_full"), 1)
                        A(h_hi[:, :, T:TT], hs[:, :, :], ACT.Copy).then_inc(sem("xT_hi"), 1)
                q = KT * (BLK[name] - BLK["BZ"]) + c
                if 4 <= q <= 20:
                    n, step = divmod(q - 4, 4)
                    if step == 0:
                        gla_gate(n)
                    if step == 1 and n < NT:
                        gla_exps(n)
                if name == "GB" and c == 4:
                    gla_out_hi(NT - 1)
                    sample_gates()
                if name == "AZ" and c == 5:
                    act.wait_ge(sem("obs_full"), 2)
                    A(x_hi[:, :, T:TT], mz[:, :, T:TT], ACT.Copy).then_inc(sem("obs_hi"), 1)
                if name == "AU" and c == 2:
                    decode_exp()
                if name == "AU" and 2 <= c <= NT + 2:
                    ln_root(c - 2)
                if name == "GA":
                    act.wait_ge(sem("mix_ready"), c + 1)
                    A(x_hi[:, c, :], t1[:, c, :], ACT.Copy).then_inc(sem("mix_hi"), 1)
                u = KT * (BLK[name] - BLK["CZ"]) + c
                if 0 <= u < 16:
                    h, step = divmod(u, 4)
                    if step == 0:
                        att_exp(h)
                    if step == 3 and h < CH - 1:
                        att_hi(h + 1)
                    if step == 1:
                        att_p(h)
                    if step == 2:
                        att_out(h)
                    if u == KT - 1:
                        act.wait_ge(sem("ocz_ready"), 1)
                        A(x_hi[:, :, T:TT], t1[:, :, T:TT], ACT.Copy).then_inc(sem("oc_hi"), 1)

            def before_evac(name, c):
                q = KT * (BLK[name] - BLK["BZ"]) + c
                if 8 <= q <= 20 and q % 4 == 0:
                    gla_norm(q // 4 - 2)
                if name == "AZ" and c == 5:
                    sample_norm()
                u = KT * (BLK[name] - BLK["CZ"]) + c
                if u == 0:
                    att_hi(0)

            def gla_gate(n):
                if n >= NT:
                    return
                act.wait_ge(sem("z_done"), n + 1)
                link(A(gl, p67[:, 0, :], ACT.Abs))
                link(A(gl, gl, ACT.Exp, scale=-1.0))
                A(gl, gl, ACT.Ln, bias=1.0).then_inc(sem("zln"), 1)

            def gla_exps(n):
                act.wait_ge(sem("cum_done"), n + 1)
                link(A(cols, p67_4[:, :, 63:256:192], ACT.Copy))
                A(eb, p67_4[:, :, 0:P], ACT.Exp).then_inc(sem("exps"), 1)
                A(enb, p67_4[:, :, 0:P], ACT.Exp, scale=-1.0).then_inc(sem("exps"), 1)
                for h in range(BH):
                    ins = A(eBl[:, h, :], p67_4[:, h, P:256], ACT.Exp, scale=-1.0, bias=cols[:, h, 1:2])
                ins.then_inc(sem("exps"), 1)
                for h in range(BH):
                    ins = A(e5[:, h, :], p67_4[:, h, 0:SUB], ACT.Exp, scale=-1.0, bias=cols[:, h, 0:1])
                ins.then_inc(sem("exps"), 1)
                A(e_last, cols[:, :, 1], ACT.Exp)
                A(eB, p67_4[:, :, P:256], ACT.Exp).then_inc(sem("exps"), 1)

            def gla_norm(n):
                if n < 0:
                    return
                if n >= 1:
                    gla_out_hi(n - 1)
                act.wait_ge(sem("o_done"), n + 1)
                for h in range(BH):
                    link(square(p67_4[:, h, :], on[:, h * BV:(h + 1) * BV], h))
                A(rstd[:, 0:BH], ssq[:, 0:BH], ACT.Sqrt, scale=1.0 / BV, bias=eps_col[:, :]).then_inc(sem("o_rt"), 1)
                act.wait_ge(sem("o_rs"), n + 1)
                for h in range(BH):
                    ins = A(on[:, h * BV:(h + 1) * BV], p67_4[:, h, :], ACT.Copy, scale=rden[:, h:h + 1])
                ins.then_inc(sem("on_ready"), 1)

            def gla_out_hi(n):
                act.wait_ge(sem("ob_full"), 2 * (n + 1))
                A(x_hi[:, :, n * P:(n + 1) * P], mz[:, :, n * P:(n + 1) * P], ACT.Copy).then_inc(sem("ob_hi"), 1)

            def sample_gates():
                act.wait_ge(sem("sz_done"), 1)
                link(A(zs, p67[:, 0, 0:BH * B].rearrange("p (h b) -> p h b", b=B), ACT.Abs))
                link(A(zs, zs, ACT.Exp, scale=-1.0))
                A(zs, zs, ACT.Ln, bias=1.0).then_inc(sem("szln"), 1)
                act.wait_ge(sem("szg"), 1)
                A(egs, egs, ACT.Exp, scale=TRI).then_inc(sem("egs_ready"), 1)

            def sample_norm():
                act.wait_ge(sem("so_done"), B)
                link(square(p67[:, 0, 0:BV], ons, 0))
                A(rstd[:, 0:1], ssq[:, 0:1], ACT.Sqrt, scale=1.0 / BV, bias=eps_col[:, :]).then_inc(sem("so_rt"), 1)
                act.wait_ge(sem("so_rs"), 1)
                A(ons, p67[:, 0, 0:BV], ACT.Copy, scale=rden[:, 0:1]).then_inc(sem("ons_ready"), 1)

            def ln_root(n):
                rows = P if n < NT else B
                act.wait_ge(sem("ln_mv"), n + 1)
                A(lstd[0:rows, :], mv[0:rows, 1:2], ACT.Sqrt, bias=eps_col[0:rows, :]).then_inc(sem("ln_rt"), 1)

            def decode_exp():
                act.wait_ge(sem("dmx"), 1)
                A(p32, p67[0:B * CH, 0, 0:MEM], ACT.Exp, scale=C_SCALE, bias=dstat[0:B * CH, 1:2],
                  accum_out=dstat[0:B * CH, 2:3]).then_inc(sem("dexp"), 1)

            def att_hi(h):
                act.wait_ge(prod_done, first("PA") + KT)
                if h == 0:
                    act.wait_ge(sem("dpv_done"), B * MT)
                if h >= 1:
                    act.wait_ge(sem("apv_done"), h)
                act.wait_ge(sem("att_loaded"), 48 * (h + 1))
                A(x_hi[:, 2 * h:2 * h + 2, 0:T], q_raw, ACT.Copy).then_inc(sem("ap_hi"), 1)
                act.wait_ge(sem("att_loaded"), 48 * (h + 1))
                A(k_hi[:, :, :], k_raw, ACT.Copy).then_inc(sem("ap_hi"), 1)
                act.wait_ge(sem("att_loaded"), 48 * (h + 1))
                A(v_hi[:, :, :], v_raw, ACT.Copy).then_inc(sem("ap_hi"), 1)

            def att_exp(h):
                act.wait_ge(sem("anmx"), h + 1)
                if h == 0:
                    act.wait_ge(sem("docs_done"), 1)
                for n in range(NT):
                    A(prob[:, n, :], p45_4[:, n, :], ACT.Exp, scale=C_SCALE, bias=nmx[:, n:n + 1],
                      accum_out=den[:, n:n + 1]).then_inc(sem("aexp"), 1)

            def att_p(h):
                act.wait_ge(sem("apT_done"), h + 1)
                A(pT_hi[:, :, :], p67[:, :, :], ACT.Copy).then_inc(sem("apT_hi"), 1)

            def att_out(h):
                act.wait_ge(sem("oc_full"), h + 1)
                A(x_hi[:, 2 * h:2 * h + 2, 0:T], t1[:, 2 * h:2 * h + 2, 0:T], ACT.Copy).then_inc(sem("oc_hi"), 1)

            for name in NAMES:
                if name == "QK":
                    act.wait_ge(sem("params_loaded"), 64)
                    A(gd_hi[:, :, :], gd_raw[:, :, :], ACT.Copy).then_inc(sem("gd_hi_ready"), 1)
                    act.wait_ge(sem("gd_ones"), 1)
                    act.wait_ge(sem("gd_done"), 1)
                    A(gdT[0:RANK, :].rearrange("p (a b) -> p a b", a=2), p45[0:RANK, :, 0:HALF], ACT.Copy).then_inc(sem("gdT_ready"), 1)
                if name == "V":
                    for s in range(2):
                        act.wait_ge(spilled["K"][s], 16 * KT // 2)
                if name == "QK":
                    act.wait_ge(sem("xT_done"), KT + 1)
                if name == "BZ":
                    act.wait_ge(sem("xT_done"), KT + 1)
                if name == "GB":
                    act.wait_ge(sem("params_loaded"), 64)
                if name == "AZ":
                    act.wait_ge(sem("sqk_taken"), 1)
                if name == "PB":
                    for s in range(2):
                        act.wait_ge(spilled["CQ"][s], 16 * KT // 2)
                if name == "AV":
                    act.wait_ge(stage_used, ST["PB"] + KT)
                if name == "AU":
                    act.wait_ge(tr_done, TR["AV"] + KT)
                if name == "GA":
                    act.wait_ge(sem("wsT_ready"), 1)
                    act.wait_ge(sem("dpT_done"), 1)
                if name == "CZ":
                    act.wait_ge(sem("mix_lo"), AH)
                    act.wait_ge(sem("mix_hi"), AH)
                if name == "GC":
                    act.wait_ge(stage_used, ST["PA"] + KT)
                if name == "OUT":
                    act.wait_ge(stage_used, ST["PC"] + KT)

                def body(it, g):
                    for j in range(4):
                        nj = (j + 2) % 4
                        hi(g + j + 2, nj, (it + 2 * BLK[name] + (1 if j < 2 else 2)) * 16)
                        if name in IRREGULAR:
                            before_evac(name, 4 * it + j)
                        evac(name, it, j, g)
                        if name == "PC":
                            c = it * 4 + j
                            act.wait_ge(sem("merged"), c + (KT + 1))
                            A(h_hi[:, bass.ds(c, 1), :], mz[:, bass.ds(c, 1), :], ACT.Copy).then_inc(sem("m_hi"), 1)
                        if name in IRREGULAR:
                            hooks(name, 4 * it + j)
                over_block(act, name, body)

            act.wait_ge(tr_used, TR["OUT"] + KT)
            act.wait_ge(sem("outs_used"), KT)
            for n in range(NT):
                link(square(tok[:, n, :], junk2, n))
            link(square(stok[:, :], junk2[0:B, :], NT))
            A(rstd[:, 0:NT], ssq[:, 0:NT], ACT.Sqrt, scale=1.0 / D, bias=eps_col[:, :]).then_inc(sem("y_rt"), 1)
            A(rstd[0:B, NT:NT + 1], ssq[0:B, NT:NT + 1], ACT.Sqrt, scale=1.0 / D, bias=eps_col[0:B, :]).then_inc(sem("y_rt"), 1)

        @block.tensor
        def _(pe):
            MM, TRP = nc.tensor.matmul, nc.tensor.transpose

            def three(out, w, x, first_mm, last_mm):
                MM(out, w[0], x[1], start=first_mm, stop=False)
                MM(out, w[1], x[0], start=False, stop=False)
                return MM(out, w[0], x[0], start=False, stop=last_mm)

            def project(name, j, t):
                pe.wait_ge(split_done, t + 1)
                wait(pe, evac_done, t - 1)
                xh, xl = (x_hi, x_lo) if name in ("K", "V", "PB", "PA", "PC") else (h_hi, h_lo)
                if name in ("K", "V"):
                    spans = [(0, MEM)]
                else:
                    spans = [(0, HALF), (HALF, TT)]
                for k in range(KT):
                    if name == "OUT" and isinstance(t, int) and t == first("OUT"):
                        pe.wait_ge(sem("m_lo"), k + 1)
                    for wp, xp in ((w_hi, xl), (w_lo, xh), (w_hi, xh)):
                        for a, (c0, c1) in enumerate(spans):
                            ins = MM(mm[:, j % 2, a, 0:c1 - c0], wp[:, j, k, :], xp[:, k, c0:c1],
                                     start=(k == 0 and wp is w_hi and xp is xl), stop=(k == KT - 1 and wp is w_hi and xp is xh))
                ins.then_inc(prod_done, 1)

            def to_tokens(name, it, j, g):
                c = it * 4 + j
                pe.wait_ge(evac_done, g + j + 1)
                wait(pe, tr_used, c + (TR[name] - 1))
                n_rows = MT if name in ("K", "V") else NT
                for n in range(n_rows):
                    ins = TRP(p45[:, j % 2, n * P:(n + 1) * P], stage[:, j % 2, n * P:(n + 1) * P], ident[:, :])
                if n_rows == NT:
                    ins = TRP(p67[0:B, j % 2, 0:P], stage[:, j % 2, T:TT], ident[:, :])
                ins.then_inc(tr_done, 1)

            def hooks(name, c):
                if name == "K":
                    if 1 <= c <= 4:
                        for k in (2 * c - 2, 2 * c - 1):
                            pe.wait_ge(sem("x_n"), NT)
                            wait(pe, sem("xT_lo"), k - 1)
                            for n in range(NT):
                                ins = TRP(p67[:, k % 2, n * P:(n + 1) * P], x_in[:, n, k * P:(k + 1) * P], ident[:, :])
                            ins.then_inc(sem("xT_done"), 1)
                    if c == 5:
                        pe.wait_ge(sem("x_n"), NT + 1)
                        pe.wait_ge(sem("xT_lo"), KT)
                        for k in range(KT):
                            ins = TRP(p67[:, 0, k * B:(k + 1) * B], xs_in[:, k * P:(k + 1) * P], ident[0:B, 0:B])
                        ins.then_inc(sem("xT_done"), 1)
                q = KT * (BLK[name] - BLK["BZ"]) + c
                if 4 <= q <= 20:
                    n, step = divmod(q - 4, 4)
                    if step == 0:
                        if n >= 1:
                            gla_turn(n - 1)
                        if n < NT:
                            gla_z(n)
                    elif step == 1:
                        gla_cum(n)
                    elif step == 2:
                        gla_scores(n)
                    else:
                        gla_out(n)
                if name == "GB" and c == 4:
                    for h in range(BH):
                        ins = MM(p67[:, 0, h * B:(h + 1) * B], w_up[:, h * P:(h + 1) * P], gdT[:, T:TT], start=(h == 0), stop=(h == BH - 1), skip_group_check=True)
                    ins.then_inc(sem("sz_done"), 1)
                if name == "GB" and c >= 5:
                    sample_out(c - 5)
                if name == "AZ" and c <= 4:
                    sample_out(c + 3)
                if name == "AZ" and c == 5:
                    pe.wait_ge(sem("ons_ready"), 1)
                    pe.wait_ge(sem("ob_full"), 2 * NT)
                    for a in range(2):
                        ins = TRP(p45[:, 0, a * P:(a + 1) * P], ons[:, a * P:(a + 1) * P], ident[:, :])
                    ins.then_inc(sem("onsT_done"), 1)
                if name == "PB" and c == 0:
                    pe.wait_ge(sem("qs_ready"), KT)
                    for k in range(KT):
                        ins = TRP(p67_8[0:B, k, :], qsT[:, k, :], ident[:, :])
                    ins.then_inc(sem("dq_T"), 1)
                if name == "AU" and c == 6:
                    pe.wait_ge(sem("ws_loaded"), 16)
                    pe.wait_ge(tr_used, TR["AV"] + KT)
                    for h in range(AH):
                        ins = TRP(p45_8[:, h, :], ws_raw[:, h, :], ident[:, :])
                    ins.then_inc(sem("wsT_done"), 1)
                if name == "GA":
                    mix(c)
                if name in ("AU", "PA", "CZ"):
                    decode(name, c)
                u = KT * (BLK[name] - BLK["CZ"]) + c
                if 0 <= u < 16:
                    h, step = divmod(u, 4)
                    if step == 0:
                        att_scores(h)
                    if step == 1:
                        pe.wait_ge(sem("ap_ready"), NT * (h + 1))
                        if h == 0:
                            pe.wait_ge(sem("ocs_ready"), 1)
                        for m in range(MT):
                            for n in range(NT):
                                ins = TRP(p67[:, m, n * P:(n + 1) * P], prob[:, n, m * P:(m + 1) * P], ident[:, :])
                        ins.then_inc(sem("apT_done"), 1)
                    if step == 2:
                        att_pv(h)

            def gla_z(n):
                if n == 0:
                    pe.wait_ge(sem("gdT_ready"), 1)
                    pe.wait_ge(sem("up_loaded"), 32)
                    pe.wait_ge(tr_used, TR["BV"] + KT)
                else:
                    pe.wait_ge(sem("on_ready"), n)
                MM(p67[:, 0, :], gdT[:, n * P:(n + 1) * P], w_up, start=True, stop=True).then_inc(sem("z_done"), 1)

            def gla_cum(n):
                pe.wait_ge(sem("gl_ready"), n + 1)
                pe.wait_ge(sem("tri_ready"), 1)
                for h in range(BH):
                    ins = MM(p67_4[:, h, :], gl[:, h * P:(h + 1) * P], tri[:, :, :], start=True, stop=True)
                ins.then_inc(sem("cum_done"), 1)

            def gla_scores(n):
                pe.wait_ge(sem("ops_ready"), 2 * n + 1)
                if n >= 1:
                    pe.wait_ge(sem("ob_full"), 2 * n)
                for h in range(BH):
                    TRP(p45[:, 0, h * P:(h + 1) * P], eBl[:, h, :], ident[:, :])
                    MM(p45[:, 1, h * P:(h + 1) * P], enb[:, h, :], eb[:, h, :], start=True, stop=True)
                pe.wait_ge(sem("ops_ready"), 2 * n + 2)
                for h in range(BH):
                    ins = MM(p67[0:SUB, 0, h * P:(h + 1) * P], e5[:, h, :], eb[:, h, :], start=True, stop=True)
                ins.then_inc(sem("sc_done"), 1)

            def gla_out(n):
                pe.wait_ge(sem("ssb_ready"), n + 1)
                if n >= 1:
                    pe.wait_ge(sem("state_ready"), n)
                for h in range(BH):
                    v = tok[:, n, h * BV:(h + 1) * BV]
                    if n >= 1:
                        MM(p67_4[:, h, :], eB[:, h, :], state[:, h, :], start=True, stop=False)
                    ins = MM(p67_4[:, h, :], ssb[:, h, :], v, start=(n == 0), stop=True)
                ins.then_inc(sem("o_done"), 1)
                for h in range(BH):
                    ins = MM(p45_4[:, h, :], ktk[:, h, :], tok[:, n, h * BV:(h + 1) * BV], start=True, stop=True)
                ins.then_inc(sem("kv_done"), 1)

            def gla_turn(n):
                pe.wait_ge(sem("on_ready"), n + 1)
                pe.wait_ge(sem("state_ready"), n + 1)
                for v in range(KT):
                    ins = TRP(p45_8[:, v, :], on[:, v * P:(v + 1) * P], ident[:, :])
                ins.then_inc(sem("onT_done"), 1)

            def sample_out(b):
                pe.wait_ge(sem("ss_ready"), BH * (b + 1))
                for h in range(BH):
                    ins = MM(p67[32 * h:32 * h + B, 0, 0:BV], qmask[:, h, b, :], s_in[:, b % 2, h, :],
                             start=(b == 0), stop=(b == B - 1), skip_group_check=True)
                ins.then_inc(sem("so_done"), 1)

            def mix(h):
                if h == 0:
                    pe.wait_ge(sem("vn_ready"), NT)
                    pe.wait_ge(sem("vns_ready"), 1)
                    pe.wait_ge(sem("wsT_ready"), 1)
                if h >= 2:
                    pe.wait_ge(sem("mix_ready"), h - 1)
                for n in range(NT):
                    MM(p45[:, h % 2, n * P:(n + 1) * P], tok[:, n, h * P:(h + 1) * P], wsT[:, h, :], start=True, stop=True)
                TRP(p67[:, h % 2, 0:B], stok[:, h * P:(h + 1) * P], ident[0:B, 0:B]).then_inc(sem("mix_done"), 1)

            def decode(name, c):
                if name == "AU" and c == 2:
                    pe.wait_ge(sem("dsc_done"), B * MT * CH)
                    pe.wait_ge(tr_used, TR["AV"] + KT)
                    pe.wait_ge(sem("stok_in"), 2 * KT)
                    for m in range(MT):
                        ins = TRP(p67[0:B * CH, 0, m * P:(m + 1) * P], sc[:, m, :], ident[:, :])
                    ins.then_inc(sem("dsT_done"), 1)
                if name == "AU" and c == 3:
                    pe.wait_ge(sem("dp_ready"), 1)
                    for m in range(MT):
                        ins = TRP(p67[:, 1, m * B * CH:(m + 1) * B * CH], p32[:, m * P:(m + 1) * P], ident[0:B * CH, 0:B * CH])
                    ins.then_inc(sem("dpT_done"), 1)
                if name == "PA" and c % 2 == 1:
                    r = c // 2
                    g, m = divmod(r, 2)
                    if r == 0:
                        pe.wait_ge(sem("mix_ready"), AH)
                        pe.wait_ge(sem("pm_ready"), 2)
                    for a in range(2):
                        for j in range(4):
                            i = 4 * r + j
                            if a == 0 and i < 2:
                                pe.wait_ge(sem("vc_loadedw"), 32)
                            elif a == 0:
                                pe.wait_ge(sem(f"vc_loaded{(i - 2) % 4}"), 16 * ((i - 2) // 4 + 1))
                            ins = MM(p45[32 * j:32 * j + 8, a, :], pz[:, m, 4 * g + j, :], v_slots[i][:, a * 512:(a + 1) * 512],
                                     start=(r == 0), stop=(r == 3), skip_group_check=True)
                            if a == 1:
                                ins.then_inc(sem("dpv_done"), 1)
                if name == "CZ" and c == 0:
                    pe.wait_ge(sem("do_ready"), 1)
                    pe.wait_ge(sem("sel_ready"), 2)
                    for k in range(KT):
                        ins = MM(p67[:, 0, k * B:(k + 1) * B], o_sb[:, k * P:(k + 1) * P], sel[:, k // 2, :, :],
                                 start=(k == 0), stop=(k == KT - 1), skip_group_check=True)
                    ins.then_inc(sem("docs_done"), 1)

            def att_scores(h):
                pe.wait_ge(sem("ap_lo"), 3 * (h + 1))
                if h >= 1:
                    pe.wait_ge(sem("oc_full"), h)
                for n in range(NT):
                    for d in range(2):
                        q = [p[:, 2 * h + d, n * P:(n + 1) * P] for p in (x_hi, x_lo)]
                        ins = three(p45_4[:, n, :], q, (k_hi[:, d, :], k_lo[:, d, :]), d == 0, d == 1)
                ins.then_inc(sem("asc_done"), 1)

            def att_pv(h):
                pe.wait_ge(sem("apT_lo"), h + 1)
                for d in range(2):
                    for m in range(MT):
                        v = [p[:, m, d * P:(d + 1) * P] for p in (v_hi, v_lo)]
                        ins = three(p45[:, d, :], v, (pT_hi[:, m, :], pT_lo[:, m, :]), m == 0, m == MT - 1)
                ins.then_inc(sem("apv_done"), 1)

            pe.wait_ge(sem("ident_ready"), 1)
            for k in range(KT):
                pe.wait_ge(sem("mem_n"), MT)
                wait(pe, sem("memT_lo"), k - 1)
                for n in range(MT):
                    ins = TRP(p45[:, k % 2, n * P:(n + 1) * P], mem_in[:, n, k * P:(k + 1) * P], ident[:, :])
                ins.then_inc(sem("memT_done"), 1)
            pe.wait_ge(sem("memT_lo"), KT)

            for name in NAMES:
                if name == "QK":
                    pe.wait_ge(sem("xT_lo"), KT + 1)
                    pe.wait_ge(sem("gd_split"), 1)
                    pe.wait_ge(tr_used, TR["V"] + KT)
                    for k in range(KT):
                        for wp, xp in ((gd_hi, h_lo), (gd_lo, h_hi), (gd_hi, h_hi)):
                            for a in range(2):
                                ins = MM(p45[:, a, 0:HALF], wp[:, k, :], xp[:, k, a * HALF:(a + 1) * HALF],
                                         start=(k == 0 and xp is h_lo), stop=(k == KT - 1 and wp is gd_hi and xp is h_hi))
                    ins.then_inc(sem("gd_done"), 1)
                if name == "BV":
                    pe.wait_ge(sem("gdT_ready"), 1)
                if name == "PB":
                    pe.wait_ge(sem("obs_ready"), 1)
                if name == "PA":
                    pe.wait_ge(sem("mix_lo"), AH)
                if name == "PC":
                    pe.wait_ge(sem("oc_lo"), CH + 1)

                def body(it, g):
                    for j in range(4):
                        project(name, j, g + j)
                        if name in TR and j >= 1:
                            to_tokens(name, it, j - 1, g)
                        if name in IRREGULAR:
                            hooks(name, 4 * it + j)
                    if name in TR:
                        to_tokens(name, it, 3, g)
                over_block(pe, name, body)

        @block.vector
        def _(dve):
            V = nc.vector
            steps = [0]

            def link(ins):
                steps[0] += 1
                ins.then_inc(sem("dve_link"), 1)
                dve.wait_ge(sem("dve_link"), steps[0])

            def f32(x):
                return x.bitcast(F32)

            def lo(t, j):
                if isinstance(t, int) and t >= NTILES:
                    return
                dve.wait_ge(hi_ready, t + 1)
                V.tensor_tensor(w_lo[:, j], raw[:, j // 2, :, (j % 2) * P:(j % 2 + 1) * P], f32(w_hi[:, j]),
                                ALU.subtract).then_inc(split_done, 1)

            def post(name, it, j, g):
                c = it * 4 + j
                cs = bass.ds(c * P, P)
                if name in TR:
                    dve.wait_ge(tr_done, c + (TR[name] + 1))
                    src = p45[:, j % 2, :].rearrange("p (n c) -> p n c", c=P)
                    if name in ("K", "V"):
                        r = 0 if name == "K" else 2
                        V.tensor_copy(tok[:, r:r + 2, cs], src[:, 0:MT, :]).then_inc(tr_used, 1)
                    elif name == "OUT":
                        V.tensor_tensor(stok[:, cs], p67[0:B, j % 2, 0:P], xs_in[:, cs], ALU.add).then_inc(sem("outs_used"), 1)
                        V.tensor_tensor(tok[:, :, cs], src, x_in[:, :, cs], ALU.add).then_inc(tr_used, 1)
                    else:
                        V.tensor_copy(stok[:, cs], p67[0:B, j % 2, 0:P]).then_inc(sem("stok_in"), 1)
                        V.tensor_copy(tok[:, :, cs], src).then_inc(tr_used, 1)
                if name in ST:
                    dve.wait_ge(evac_done, g + j + 1)
                    s = stage[:, j % 2, :]
                    row = bass.ds(c, 1)
                    if name == "AU":
                        V.tensor_tensor(t1[:, c, :], t1[:, c, :], s, ALU.mult).then_inc(stage_used, 1)
                    if name == "PB":
                        V.tensor_tensor(mz[:, c, :], gate[:, c, :], s, ALU.mult).then_inc(stage_used, 1)
                    if name in ("PA", "PC"):
                        g2 = gate[:, row, :].rearrange("p o t -> p (o t)")
                        m2 = mz[:, row, :].rearrange("p o t -> p (o t)")
                        V.tensor_tensor(g2, g2, s, ALU.mult).then_inc(stage_used, 1)
                        dve.wait_ge(stage_used, c + (ST[name] + 1))
                        V.tensor_tensor(m2, m2, g2, ALU.add).then_inc(sem("merged"), 1)
                    if name == "PC":
                        dve.wait_ge(sem("m_hi"), c + 1)
                        V.tensor_tensor(h_lo[:, row, :], mz[:, row, :], f32(h_hi[:, row, :]), ALU.subtract).then_inc(sem("m_lo"), 1)

            def hooks(name, c):
                if name == "K":
                    if c == 0:
                        dve.wait_ge(sem("rt_x"), 2)
                        link(V.reciprocal(rstd[:, 0:NT], rstd[:, 0:NT]))
                        link(V.reciprocal(rstd[0:B, NT:NT + 1], rstd[0:B, NT:NT + 1]))
                        for n in range(NT):
                            V.tensor_scalar(x_in[:, n, :], x_in[:, n, :], rstd[:, n:n + 1], None, ALU.mult).then_inc(sem("x_n"), 1)
                        V.tensor_scalar(xs_in, xs_in, rstd[0:B, NT:NT + 1], None, ALU.mult).then_inc(sem("x_n"), 1)
                    elif c <= 4:
                        for k in (2 * c - 2, 2 * c - 1):
                            dve.wait_ge(sem("xT_hi"), k + 1)
                            V.scalar_tensor_tensor(out=h_lo[:, k, 0:T], in0=p67[:, k % 2, :], scalar=gn1[:, k:k + 1],
                                                   in1=f32(h_hi[:, k, 0:T]), op0=ALU.mult, op1=ALU.subtract).then_inc(sem("xT_lo"), 1)
                    elif c == 5:
                        dve.wait_ge(sem("xT_done"), KT + 1)
                        V.tensor_tensor(hs[:, :, :], p67[:, 0, 0:KT * B].rearrange("p (k b) -> p k b", b=B),
                                        gn1[:, :].unsqueeze(2).broadcast_to([P, KT, B]), ALU.mult).then_inc(sem("xsT_full"), 1)
                        dve.wait_ge(sem("xT_hi"), KT + 1)
                        V.tensor_tensor(h_lo[:, :, T:TT], hs[:, :, :], f32(h_hi[:, :, T:TT]), ALU.subtract).then_inc(sem("xT_lo"), 1)
                q = KT * (BLK[name] - BLK["BZ"]) + c
                if 4 <= q <= 20:
                    n, step = divmod(q - 4, 4)
                    if step == 0:
                        if n >= 1:
                            dve.wait_ge(sem("o_rt"), n)
                            V.reciprocal(rden[:, 0:BH], rstd[:, 0:BH]).then_inc(sem("o_rs"), 1)
                            if n >= 2:
                                gla_out_lo(n - 2)
                            gla_full(n - 1)
                        if n < NT:
                            gla_gates(n)
                    elif step == 1:
                        gla_ops(n)
                    elif step == 2:
                        gla_masks(n)
                    else:
                        gla_state(n)
                if name == "GB" and c == 4:
                    gla_out_lo(NT - 1)
                    sample_prepare()
                if name == "GB" and c >= 5:
                    sample_state(c - 5)
                if name == "AZ" and c <= 4:
                    sample_state(c + 3)
                if name == "AZ" and c == 5:
                    dve.wait_ge(sem("so_rt"), 1)
                    V.reciprocal(rden[:, 0:1], rstd[:, 0:1]).then_inc(sem("so_rs"), 1)
                    dve.wait_ge(sem("onsT_done"), 1)
                    for a in range(2):
                        m = mz[:, a:KT:2, T:TT]
                        o = p45[:, 0, a * P:(a + 1) * P].rearrange("p (h c) -> p h c", c=32)[:, :, 0:B]
                        V.scalar_tensor_tensor(out=m, in0=o, scalar=gnc[:, a:a + 1], in1=m,
                                               op0=ALU.mult, op1=ALU.mult).then_inc(sem("obs_full"), 1)
                    dve.wait_ge(sem("obs_hi"), 1)
                    V.tensor_tensor(x_lo[:, :, T:TT], mz[:, :, T:TT], f32(x_hi[:, :, T:TT]), ALU.subtract).then_inc(sem("obs_ready"), 1)
                if name == "PB" and c == 1:
                    dve.wait_ge(sem("dq_T"), 1)
                    V.tensor_copy(work[0:B, 2048:2048 + D].rearrange("p (a b) -> p a b", a=2), p67[0:B, :, :]).then_inc(sem("dq_ready"), 1)
                if name == "AV" and c >= 1:
                    decode_scores(range(max(0, 2 * c - 3), 2 * c - 1))
                if name == "AU":
                    if c == 6:
                        dve.wait_ge(sem("wsT_done"), 1)
                        dve.wait_ge(sem("st_stored"), 16)
                        V.scalar_tensor_tensor(out=wsT, in0=p45_8, scalar=1.0 / TRI, in1=tri[:, 1:2, :].broadcast_to([P, AH, P]),
                                               op0=ALU.mult, op1=ALU.mult).then_inc(sem("wsT_ready"), 1)
                    if c == 0:
                        decode_scores((13, 14))
                    if c == 1:
                        decode_scores((15,))
                    if c == 2:
                        decode_softmax()
                    if c == 3:
                        dve.wait_ge(sem("dpT_done"), 1)
                        dve.wait_ge(sem("sel_ready"), 1)
                        pT = p67[:, 1, 0:MT * B * CH].rearrange("p (m b h) -> p m b h", b=B, h=CH)
                        for g in range(2):
                            V.tensor_copy(pz[:, :, 4 * g:4 * g + 4, 4 * g:4 * g + 4], pT[:, :, 4 * g:4 * g + 4, :]).then_inc(sem("pm_ready"), 1)
                    if 2 <= c <= NT + 2:
                        layer_norm(c - 2)
                if name == "GA":
                    mix(c)
                if name == "PA" and c == 7:
                    dve.wait_ge(sem("dpv_done"), B * MT)
                    V.tensor_copy(o_sb.rearrange("p (a b) -> p a b", a=2), p45[:, :, :]).then_inc(sem("do_ready"), 1)
                if name == "CZ" and c == 0:
                    att_lo(0)
                    dve.wait_ge(sem("docs_done"), 1)
                    V.tensor_copy(ocs[:, :, :], p67[:, 0, 0:KT * B].rearrange("p (k b) -> p k b", b=B)).then_inc(sem("ocs_ready"), 1)
                u = KT * (BLK[name] - BLK["CZ"]) + c
                if 0 <= u < 16:
                    h, step = divmod(u, 4)
                    if step == 0:
                        att_soft(h)
                    if step == 3 and h < CH - 1:
                        att_lo(h + 1)
                    if step == 1:
                        dve.wait_ge(sem("apT_hi"), h + 1)
                        V.tensor_tensor(pT_lo[:, :, :], p67[:, :, :], f32(pT_hi[:, :, :]), ALU.subtract).then_inc(sem("apT_lo"), 1)
                    if step == 2:
                        dve.wait_ge(sem("apv_done"), h + 1)
                        dve.wait_ge(evac_done, first("CZ") + 2 * h + 2)
                        tc = t1[:, 2 * h:2 * h + 2, 0:T]
                        V.tensor_tensor(tc, p45[:, :, :], tc, ALU.mult).then_inc(sem("oc_full"), 1)
                        n_hi = h + 1 if h < 2 else h + 2
                        dve.wait_ge(sem("oc_hi"), n_hi)
                        V.tensor_tensor(x_lo[:, 2 * h:2 * h + 2, 0:T], tc, f32(x_hi[:, 2 * h:2 * h + 2, 0:T]), ALU.subtract).then_inc(sem("oc_lo"), 1)
                    if u == KT - 1:
                        dve.wait_ge(evac_done, first("CZ") + KT)
                        V.tensor_tensor(t1[:, :, T:TT], t1[:, :, T:TT], ocs[:, :, :], ALU.mult).then_inc(sem("ocz_ready"), 1)
                        dve.wait_ge(sem("oc_hi"), 3)
                        V.tensor_tensor(x_lo[:, :, T:TT], t1[:, :, T:TT], f32(x_hi[:, :, T:TT]), ALU.subtract).then_inc(sem("oc_lo"), 1)

            def gla_gates(n):
                dve.wait_ge(sem("zln"), n + 1)
                V.scalar_tensor_tensor(out=gl, in0=p67[:, 0, :], scalar=0.0, in1=gl, op0=ALU.min,
                                       op1=ALU.subtract).then_inc(sem("gl_ready"), 1)

            def gla_ops(n):
                q = t1[:, 0:BH, n * P:(n + 1) * P]
                k = t1[:, BH:2 * BH, n * P:(n + 1) * P]
                dve.wait_ge(sem("exps"), 5 * n + 1)
                dve.wait_ge(evac_done, first("QK") + KT)
                V.scalar_tensor_tensor(out=eb, in0=q, scalar=Q_SCALE, in1=eb, op0=ALU.mult, op1=ALU.mult)
                dve.wait_ge(sem("exps"), 5 * n + 2)
                V.tensor_tensor(enb, k, enb, ALU.mult)
                dve.wait_ge(sem("exps"), 5 * n + 3)
                V.tensor_tensor(eBl, k, eBl, ALU.mult)
                dve.wait_ge(sem("exps"), 5 * n + 4)
                V.tensor_tensor(e5, k[:, :, 0:SUB], e5, ALU.mult).then_inc(sem("ops_ready"), 1)
                dve.wait_ge(sem("exps"), 5 * n + 5)
                V.scalar_tensor_tensor(out=eB, in0=q, scalar=Q_SCALE, in1=eB, op0=ALU.mult, op1=ALU.mult).then_inc(sem("ops_ready"), 1)

            def gla_masks(n):
                dve.wait_ge(sem("sc_done"), n + 1)
                V.tensor_copy(ktk, p45[:, 0, :].rearrange("p (h c) -> p h c", c=P))
                link(V.scalar_tensor_tensor(out=ssb, in0=p45[:, 1, :].rearrange("p (h c) -> p h c", c=P), scalar=1.0 / TRI,
                                            in1=tri[:, 0:1, :].broadcast_to([P, BH, P]), op0=ALU.mult, op1=ALU.mult))
                V.tensor_copy(ssb[0:SUB, :, SUB:P], p67[0:SUB, 0, :].rearrange("p (h c) -> p h c", c=P)[:, :, SUB:P]).then_inc(sem("ssb_ready"), 1)

            def gla_state(n):
                dve.wait_ge(sem("kv_done"), n + 1)
                if n == 0:
                    V.tensor_copy(state[:, :, :], p45_4).then_inc(sem("state_ready"), 1)
                else:
                    for h in range(BH):
                        ins = V.scalar_tensor_tensor(out=state[:, h, :], in0=state[:, h, :], scalar=e_last[:, h:h + 1],
                                                     in1=p45_4[:, h, :], op0=ALU.mult, op1=ALU.add)
                    ins.then_inc(sem("state_ready"), 1)

            def gla_full(n):
                dve.wait_ge(sem("onT_done"), n + 1)
                if n == 0:
                    dve.wait_ge(sem("params_loaded"), 64)
                    dve.wait_ge(evac_done, first("BZ") + KT)
                for a in range(2):
                    m = mz[:, a:KT:2, n * P:(n + 1) * P]
                    V.scalar_tensor_tensor(out=m, in0=p45_8[:, a:KT:2, :], scalar=gnc[:, a:a + 1], in1=m,
                                           op0=ALU.mult, op1=ALU.mult).then_inc(sem("ob_full"), 1)

            def gla_out_lo(n):
                dve.wait_ge(sem("ob_hi"), n + 1)
                s = slice(n * P, (n + 1) * P)
                V.tensor_tensor(x_lo[:, :, s], mz[:, :, s], f32(x_hi[:, :, s]), ALU.subtract)

            def sample_prepare():
                dve.wait_ge(sem("sz_done"), 1)
                link(V.memset(qmask.rearrange("p h b c -> p (h b c)"), 0.0))
                V.tensor_scalar(qmask.rearrange("p h b c -> p h (b c)")[:, :, 0:B * B:B + 1], t1[:, 0:BH, T:TT], Q_SCALE, None,
                                ALU.mult)
                V.tensor_copy(ksT[:, :, :], t1[:, BH:2 * BH, T:TT]).then_inc(sem("sqk_taken"), 1)
                dve.wait_ge(sem("szln"), 1)
                V.scalar_tensor_tensor(out=egs, in0=p67[:, 0, 0:BH * B].rearrange("p (h b) -> p h b", b=B), scalar=0.0,
                                       in1=zs, op0=ALU.min, op1=ALU.subtract).then_inc(sem("szg"), 1)

            def sample_state(b):
                s = b % 2
                dve.wait_ge(sem(f"ss_loaded{s}"), 32 * (b // 2 + 1))
                if b == 0:
                    dve.wait_ge(sem("egs_ready"), 1)
                    dve.wait_ge(sem("sqk_taken"), 1)
                else:
                    dve.wait_ge(sem("ss_ready"), BH * b)
                for h in range(BH):
                    V.tensor_scalar(tmp_kv[:, h, :], v_bc[:, s, h * BV:(h + 1) * BV], ksT[:, h, b:b + 1], None, ALU.mult).then_inc(sem("tmp_kv"), 1)
                for h in range(BH):
                    dve.wait_ge(sem("tmp_kv"), BH * b + h + 1)
                    V.scalar_tensor_tensor(out=s_in[:, s, h, :], in0=s_in[:, s, h, :], scalar=egs[:, h, b:b + 1],
                                           in1=tmp_kv[:, h, :], op0=ALU.mult, op1=ALU.add).then_inc(sem("ss_ready"), 1)

            def layer_norm(n):
                rows, r = (tok[:, n, :], P) if n < NT else (stok[:, :], B)
                if n == 0:
                    dve.wait_ge(tr_used, TR["AV"] + KT)
                    dve.wait_ge(sem("stok_in"), 2 * KT)
                for a in range(2):
                    link(V.bn_stats(stats[0:r, a, :], rows[:, a * 512:(a + 1) * 512]))
                V.bn_aggr(mv[0:r, :], stats[0:r, :, :]).then_inc(sem("ln_mv"), 1)
                dve.wait_ge(sem("ln_rt"), n + 1)
                link(V.reciprocal(lrst[0:r, :], lstd[0:r, :]))
                V.tensor_scalar(rows, rows, mv[0:r, 0:1], lrst[0:r, :], ALU.subtract, ALU.mult).then_inc(sem("ln_norm"), 1)
                if n == NT:
                    dve.wait_ge(sem("ln_norm"), NT + 1)
                    dve.wait_ge(sem("a_loaded"), 48)
                    link(V.tensor_tensor(rows, rows, lng[0:B, :], ALU.mult))
                    V.tensor_tensor(rows, rows, lnb[0:B, :], ALU.add).then_inc(sem("vns_ready"), 1)

            def mix(h):
                dve.wait_ge(sem("mix_done"), h + 1)
                if h == 0:
                    dve.wait_ge(sem("a_loaded"), 48)
                    dve.wait_ge(sem("params_loaded"), 64)
                V.tensor_tensor(mtmp[:, 0:T].rearrange("p (n t) -> p n t", t=P), p45[:, h % 2, :].rearrange("p (n t) -> p n t", t=P),
                                bs_bc[:, h:h + 1, :].broadcast_to([P, NT, P]), ALU.add)
                link(V.tensor_scalar(mtmp[:, T:TT], p67[:, h % 2, 0:B], w00[:, h:h + 1], bs_bc[:, h, 0:1], ALU.mult, ALU.add))
                V.tensor_tensor(t1[:, h, :], t1[:, h, :], mtmp, ALU.mult).then_inc(sem("mix_ready"), 1)
                dve.wait_ge(sem("mix_hi"), h + 1)
                V.tensor_tensor(x_lo[:, h, :], t1[:, h, :], f32(x_hi[:, h, :]), ALU.subtract).then_inc(sem("mix_lo"), 1)

            def decode_scores(tiles):
                for i in tiles:
                    b, m = divmod(i, MT)
                    dve.wait_ge(sem(f"kc_loaded{i % 2}"), 16 * (i // 2 + 1))
                    if m == 0:
                        dve.wait_ge(sem(f"qb_loaded{b % 2}"), 16 * (b // 2 + 1))
                    for h in range(CH):
                        k = kc[:, i % 2, h * CD:(h + 1) * CD]
                        V.tensor_tensor_reduce(k, k, q_bc[:, b % 2, h * CD:(h + 1) * CD], 1.0, 0.0, ALU.mult, ALU.add,
                                               sc[:, m, b * CH + h:b * CH + h + 1]).then_inc(sem("dsc_done"), 1)

            def decode_softmax():
                n = B * CH
                dve.wait_ge(sem("dsT_done"), 1)
                link(V.tensor_reduce(dstat[0:n, 0:1], p67[0:n, 0, 0:MEM], AX_X, ALU.max))
                V.tensor_scalar(dstat[0:n, 1:2], dstat[0:n, 0:1], -C_SCALE, None, ALU.mult).then_inc(sem("dmx"), 1)
                dve.wait_ge(sem("dexp"), 1)
                link(V.reciprocal(dstat[0:n, 3:4], dstat[0:n, 2:3]))
                V.tensor_scalar(p32, p32, dstat[0:n, 3:4], None, ALU.mult).then_inc(sem("dp_ready"), 1)

            def att_lo(h):
                for n, (dst, src, top) in enumerate(((x_lo[:, 2 * h:2 * h + 2, 0:T], q_raw, x_hi[:, 2 * h:2 * h + 2, 0:T]),
                                                     (k_lo[:, :, :], k_raw, k_hi[:, :, :]), (v_lo[:, :, :], v_raw, v_hi[:, :, :]))):
                    dve.wait_ge(sem("ap_hi"), 3 * h + n + 1)
                    V.tensor_tensor(dst, src, f32(top), ALU.subtract).then_inc(sem("ap_lo"), 1)

            def att_soft(h):
                dve.wait_ge(sem("asc_done"), h + 1)
                link(V.tensor_reduce(mx, p45_4, AX_X, ALU.max))
                V.tensor_scalar(nmx, mx, -C_SCALE, None, ALU.mult).then_inc(sem("anmx"), 1)
                dve.wait_ge(sem("aexp"), NT * (h + 1))
                link(V.reciprocal(rden, den))
                for n in range(NT):
                    V.tensor_scalar(prob[:, n, :], prob[:, n, :], rden[:, n:n + 1], None, ALU.mult).then_inc(sem("ap_ready"), 1)

            V.memset(eps_col, EPS).then_inc(sem("eps_ready"), 1)
            V.memset(gdT, 1.0).then_inc(sem("gd_ones"), 1)
            dve.wait_ge(sem("rt_mem"), 1)
            link(V.reciprocal(rstd[:, 0:MT], rstd[:, 0:MT]))
            for n in range(MT):
                V.tensor_scalar(mem_in[:, n, :], mem_in[:, n, :], rstd[:, n:n + 1], None, ALU.mult).then_inc(sem("mem_n"), 1)
            lo(0, 0)
            lo(1, 1)
            dve.wait_ge(sem("start_loaded"), 48)
            for k in range(KT):
                dve.wait_ge(sem("memT_hi"), k + 1)
                V.scalar_tensor_tensor(out=x_lo[:, k, 0:MEM], in0=p45[:, k % 2, 0:MEM], scalar=gm1[:, k:k + 1],
                                       in1=f32(x_hi[:, k, 0:MEM]), op0=ALU.mult, op1=ALU.subtract).then_inc(sem("memT_lo"), 1)
            dve.wait_ge(sem("start_loaded"), 48)

            for name in NAMES:
                if name == "QK":
                    dve.wait_ge(sem("gd_hi_ready"), 1)
                    V.tensor_tensor(gd_lo[:, :, :], gd_raw[:, :, :], f32(gd_hi[:, :, :]), ALU.subtract).then_inc(sem("gd_split"), 1)
                if name == "BV":
                    dve.wait_ge(sem("kv_stored"), 32)
                    dve.wait_ge(sem("kv_stored"), 32)
                if name == "AV":
                    dve.wait_ge(sem("ss_stored0"), 16 * B // 2)
                    dve.wait_ge(sem("ss_stored1"), 16 * B // 2)
                if name == "OUT":
                    dve.wait_ge(sem("end_loaded"), 48)
                    dve.wait_ge(sem("end_loaded"), 48)
                    dve.wait_ge(sem("vns_stored"), 16)

                def body(it, g):
                    for j in range(4):
                        lo(g + j + 2, (j + 2) % 4)
                        post(name, it, j, g)
                        if name in IRREGULAR:
                            hooks(name, 4 * it + j)
                over_block(dve, name, body)

            dve.wait_ge(sem("y_rt"), 2)
            dve.wait_ge(sem("end_loaded"), 48)
            link(V.reciprocal(rstd[:, 0:NT], rstd[:, 0:NT]))
            link(V.reciprocal(rstd[0:B, NT:NT + 1], rstd[0:B, NT:NT + 1]))
            for n in range(NT):
                V.scalar_tensor_tensor(out=tok[:, n, :], in0=tok[:, n, :], scalar=rstd[:, n:n + 1], in1=gf_bc,
                                       op0=ALU.mult, op1=ALU.mult).then_inc(sem("y_ready"), 1)
            V.scalar_tensor_tensor(out=stok[:, :], in0=stok[:, :], scalar=rstd[0:B, NT:NT + 1], in1=gf_bc[0:B, :],
                                   op0=ALU.mult, op1=ALU.mult).then_inc(sem("y_ready"), 1)


_INS = ['x_prompt', 'x_sample', 'state_gla', 'cache_mem_k', 'cache_mem_v', 'mem_prompt', 'g_norm', 'w_in',
        'b_gate', 'w_s', 'b_s', 'ln_v_g', 'ln_v_b', 'w_g_up', 'b_g', 'gn_g', 'g_mem', 'w_mem_kv', 'w_branch',
        'w_out', 'g_final']
_OUTS = [((1, 512, 1024), 'float32'), ((8, 1, 1024), 'float32'), ((1, 1, 4, 128, 256), 'float32'),
         ((1, 1, 256, 4, 256), 'float32'), ((1, 1, 256, 4, 256), 'float32'), ((1, 8, 4, 128, 256), 'float32'),
         ((1, 8, 1, 8, 128), 'float32')]


def kernel(**inputs):
    import numpy as _np
    import concourse.bacc as _bacc
    from concourse import mybir as _mybir
    from concourse.bass_utils import run_bass_kernel_spmd as _run

    nc = _bacc.Bacc("TRN2", target_bir_lowering=False, num_devices=1)
    arrays, args = {}, []
    for name in _INS:
        a = _np.ascontiguousarray(inputs[name])
        arrays[f"in_{name}_dram"] = a
        args.append(nc.dram_tensor(f"in_{name}_dram", a.shape, _mybir.dt.from_np(a.dtype), kind="ExternalInput").ap())
    for i, (shape, dtype) in enumerate(_OUTS):
        dt = _mybir.dt.from_np(_np.dtype(dtype))
        args.append(nc.dram_tensor(f"out_{i}_dram", shape, dt, kind="ExternalOutput").ap())
    bass_gated_parallel_step(nc, *args)
    r = _run(nc, [arrays], core_ids=[0])
    return tuple(r.results[0][f"out_{i}_dram"] for i in range(len(_OUTS)))
```

```python
from contextlib import ExitStack

import concourse.bass as bass
from concourse import mybir

ALU = mybir.AluOpType
ACT = mybir.ActivationFunctionType
F32 = mybir.dt.float32
F32R = mybir.dt.float32r
AX_X = mybir.AxisListType.X

P = 128
D = 1024
KT = D // P
T = 512
NT = T // P
B = 8
TT = T + B
HALF = TT // 2
MEM = 256
MT = MEM // P
BH, BK, BV = 4, 128, 256
CH = 4
CD = 256
AH = 8
RANK = 16
SUB = 64
EPS = 1e-6
Q_SCALE = BK ** -0.5
C_SCALE = CD ** -0.5
TRI = 1.0 / 16.0

O_AU, O_AV, O_AZ = 0, D, 2 * D
O_QK = 3 * D
O_BV = O_QK + D
O_GD = O_BV + D
O_BZ = O_GD + RANK
O_CQ = O_BZ + D
O_CZ = O_CQ + D
O_GA = O_CZ + D
O_GB = O_GA + D
O_GC = O_GB + D

NAMES = ["K", "V", "QK", "BV", "BZ", "CQ", "GB", "AZ", "PB", "AV", "AU", "GA", "PA", "CZ", "GC", "PC", "OUT"]
BLK = {n: i for i, n in enumerate(NAMES)}
NTILES = KT * len(NAMES)
XN = 5
TR = {n: KT * i for i, n in enumerate(["K", "V", "BV", "AV", "OUT"])}
ST = {n: KT * i for i, n in enumerate(["PB", "AU", "PA", "PC"])}
IRREGULAR = {"K", "V", "BZ", "CQ", "GB", "AZ", "PB", "AV", "AU", "GA", "PA", "CZ", "GC", "OUT"}


def first(name):
    return KT * BLK[name]


def wait(eng, sem, value):
    if isinstance(value, int) and value <= 0:
        return
    eng.wait_ge(sem, value)


def over_block(eng, name, body):
    if name in IRREGULAR:
        for it in range(2):
            body(it, first(name) + 4 * it)
    else:
        with eng.Fori(0, 2) as it:
            body(it, it * 4 + first(name))


def bass_gated_parallel_step(nc, x_prompt, x_sample, state_gla, cache_mem_k, cache_mem_v,
                             mem_prompt, g_norm, w_in, b_gate, w_s, b_s, ln_v_g, ln_v_b, w_g_up,
                             b_g, gn_g, g_mem, w_mem_kv, w_branch, w_out, g_final,
                             y_prompt, y_sample, st_prompt, k_prompt, v_prompt, st_sample,
                             vn_sample):
    scr_kT = nc.dram_tensor("scr_kT", [P, KT, MEM], F32, kind="Internal").ap()
    scr_qT = nc.dram_tensor("scr_qT", [P, KT, T], F32, kind="Internal").ap()
    scr_v = nc.dram_tensor("scr_v", [B, D], F32, kind="Internal").ap()
    scr_q = nc.dram_tensor("scr_q", [B, D], F32, kind="Internal").ap()

    win = w_in[0]
    source = {
        "K": w_mem_kv[0][:, 0:D], "V": w_mem_kv[0][:, D:2 * D],
        "QK": win[:, O_QK:O_QK + D], "BV": win[:, O_BV:O_BV + D], "BZ": win[:, O_BZ:O_BZ + D],
        "CQ": win[:, O_CQ:O_CQ + D], "GB": win[:, O_GB:O_GB + D], "AZ": win[:, O_AZ:O_AZ + D],
        "PB": w_branch[0, 1], "AV": win[:, O_AV:O_AV + D], "AU": win[:, O_AU:O_AU + D],
        "GA": win[:, O_GA:O_GA + D], "PA": w_branch[0, 0], "CZ": win[:, O_CZ:O_CZ + D],
        "GC": win[:, O_GC:O_GC + D], "PC": w_branch[0, 2], "OUT": w_out[0],
    }

    with ExitStack() as ctx:
        def sb(name, shape, dt=F32):
            return ctx.enter_context(nc.sbuf_tensor(name, shape, dt))

        def overlay(*layouts):
            out = []
            for n, layout in enumerate(layouts):
                own = ExitStack()
                out.append([own.enter_context(nc.sbuf_tensor(*t)) for t in layout])
                if n < len(layouts) - 1:
                    own.close()
                else:
                    ctx.enter_context(own)
            return out

        sems = {}

        def sem(name):
            if name not in sems:
                sems[name] = ctx.enter_context(nc.semaphore(name))
            return sems[name]

        h_hi = sb("h_hi", [P, KT, TT], F32R)
        h_lo = sb("h_lo", [P, KT, TT], F32R)
        x_hi = sb("x_hi", [P, KT, TT], F32R)
        x_lo = sb("x_lo", [P, KT, TT], F32R)
        gate = sb("gate", [P, KT, TT])
        mz = sb("mz", [P, KT, TT])
        t1 = sb("t1", [P, KT, TT])
        raw = sb("raw", [P, 2, KT, 2 * P])
        w_hi = sb("w_hi", [P, 4, KT, P], F32R)
        w_lo = sb("w_lo", [P, 4, KT, P], F32R)
        stage = sb("stage", [P, 2, TT])
        (att, (tok,)) = overlay(
            [("k_hi", [P, 2, MEM], F32R), ("k_lo", [P, 2, MEM], F32R),
             ("v_hi", [P, MT, CD], F32R), ("v_lo", [P, MT, CD], F32R),
             ("pT_hi", [P, MT, T], F32R), ("pT_lo", [P, MT, T], F32R)],
            [("tok", [P, NT, D], F32)])
        k_hi, k_lo, v_hi, v_lo, pT_hi, pT_lo = att
        ((gd_hi, gd_lo, gd_raw), (work,)) = overlay(
            [("gd_hi", [P, KT, P], F32R), ("gd_lo", [P, KT, P], F32R), ("gd_raw", [P, KT, P], F32)],
            [("work", [P, 3840], F32)])
        state = sb("state", [P, BH, BV])
        stok = sb("stok", [B, D])
        ident = sb("ident", [P, P])
        tri = sb("tri", [P, 2, P])
        gn1 = sb("gn1", [P, KT])
        gm1 = sb("gm1", [P, KT])
        bg1 = sb("bg1", [P, 3 * KT])
        gnc = sb("gnc", [P, 2])
        small = sb("small", [P, 96])
        qsT = sb("qsT", [P, KT, B])
        hs = sb("hs", [P, KT, B])
        ksT = sb("ksT", [P, BH, B])
        ocs = sb("ocs", [P, KT, B])
        w00 = sb("w00", [P, AH])
        ssq, rstd = small[:, 0:8], small[:, 8:16]
        cols = small[:, 16:24].rearrange("p (h c) -> p h c", c=2)
        e_last = small[:, 24:28]
        mx, nmx, den, rden = small[:, 28:32], small[:, 32:36], small[:, 36:40], small[:, 40:44]
        stats = small[:, 44:56].rearrange("p (a c) -> p a c", c=6)
        mv = small[:, 56:58]
        lstd = small[:, 58:59]
        lrst = small[:, 59:60]
        kss_last = small[:, 60:64]
        dstat = small[:, 64:70]
        eps_col = small[:, 70:71]

        def piece(base, at, shape):
            n = 1
            for s in shape:
                n *= s
            v = base[:, at:at + n]
            if len(shape) == 2:
                v = v.rearrange("p (a b) -> p a b", b=shape[1])
            if len(shape) == 3:
                v = v.rearrange("p (a b c) -> p a b c", b=shape[1], c=shape[2])
            return v

        eb = piece(work, 0, (BH, P))
        enb = piece(work, 512, (BH, P))
        eB = piece(work, 1024, (BH, P))
        eBl = piece(work, 1536, (BH, P))
        e5 = piece(work, 2048, (BH, SUB))
        gl = piece(work, 2304, (512,))
        ktk = piece(work, 2816, (BH, P))
        ssb = piece(work, 3328, (BH, P))
        on = piece(work, 0, (D,))
        tok_flat = tok[:, :, :].rearrange("p n d -> p (n d)")
        s_in = piece(tok_flat, 0, (4, BH, BV))
        egs = piece(work, 0, (BH, B))
        zs = piece(work, 32, (BH, B))
        qmask = piece(work, 64, (BH, B, B))
        ons = piece(work, 512, (BV,))
        tmp_kv = piece(work, 768, (BH, BV))
        v_bc = [stage[:, :, :].rearrange("p s t -> p (s t)")[:, 0:D], work[:, 1792:1792 + D]]
        lng = piece(work, 0, (D,))
        lnb = piece(work, D, (D,))
        bs_bc = piece(work, 2 * D, (AH, P))
        mtmp = piece(work, 3 * D, (TT,))
        wsT = state[:, :, :].rearrange("p h v -> p (h v)").rearrange("p (h t) -> p h t", t=P)
        gate_flat = gate[:, :, :].rearrange("p k t -> p (k t)")
        mz_flat = mz[:, :, :].rearrange("p k t -> p (k t)")
        t1_flat = t1[:, :, :].rearrange("p k t -> p (k t)")
        ws_raw = piece(gate_flat, 0, (AH, P))
        w_up = gate[0:RANK + 1, 6, 0:512]
        gdT = gate[0:RANK + 1, 7, :]
        mem_in = piece(gate_flat, 0, (MT, D))
        xs_in = mz_flat[0:B, 0:D]
        junk = mz_flat[:, D:2 * D]
        x_in = piece(t1_flat, 0, (NT, D))
        kc = piece(gate_flat, 0, (4, D))
        q_bc = piece(work, 0, (3, D))
        p32 = gate_flat[0:B * CH, 2 * D:2 * D + MEM]
        pz = piece(work, 3592, (MT, B, 2 * CH))
        sc = piece(work, 3744, (MT, B * CH))
        sel = piece(work, 3808, (CH, 2, 4))
        o_sb = piece(work, 2 * D, (D,))
        v_slots = [work[:, 0:D], work[:, D:2 * D]] + [tok[:, (i - 2) % 4, :] for i in range(2, B * MT)]
        q_raw = piece(work, 0, (2, T))
        k_raw = piece(work, 1024, (2, MEM))
        v_raw = piece(work, 1536, (MT, CD))
        prob = piece(work, 2048, (NT, MEM))
        gf_bc = piece(work, 0, (D,))
        osq = piece(work, 2 * D, (NT + 1, KT))
        junk2 = piece(work, D, (NT + 1, P))

        mm = ctx.enter_context(nc.psum_tensor("mm", [P, 2, 2, 512], F32))
        p45 = ctx.enter_context(nc.psum_tensor("p45", [P, 2, 512], F32))
        p67 = ctx.enter_context(nc.psum_tensor("p67", [P, 2, 512], F32))
        p45_8 = p45[:, :, :].rearrange("p a (b c) -> p (a b) c", c=P)
        p67_8 = p67[:, :, :].rearrange("p a (b c) -> p (a b) c", c=P)
        p45_4 = p45[:, :, :].rearrange("p a (b c) -> p (a b) c", c=256)
        p67_4 = p67[:, :, :].rearrange("p a (b c) -> p (a b) c", c=256)

        def mem_bank(k):
            return (p45, p67)[k // 2 % 2][:, k % 2, 0:MEM]

        w_loaded = [sem("w_loaded0"), sem("w_loaded1")]
        hi_ready = sem("hi_ready")
        split_done = sem("split_done")
        prod_done = sem("prod_done")
        evac_done = sem("evac_done")
        tr_done = sem("tr_done")
        tr_used = sem("tr_used")
        stage_used = sem("stage_used")
        spilled = {n: [sem(f"{n}_spilled0"), sem(f"{n}_spilled1")] for n in ("K", "CQ")}

        ring_states = B // 4
        ring_keys = ring_states + B * MT // 4
        row_v = [B // 2, B // 2, 0]

        block = ctx.enter_context(nc.Block())

        @block.sync
        def _(sp):
            sp.dma_start(mem_in, mem_prompt[0].rearrange("(n p) d -> p n d", p=P)).then_inc(sem("mem_loaded"), 16)
            sp.dma_start(raw[:, 0], source["K"][:, 0:256].rearrange("(k p) c -> p k c", p=P)).then_inc(w_loaded[0], 16)
            sp.dma_start(raw[:, 1], source["K"][:, 256:512].rearrange("(k p) c -> p k c", p=P)).then_inc(w_loaded[1], 16)
            sp.dma_start(x_in, x_prompt[0].rearrange("(n p) d -> p n d", p=P)).then_inc(sem("x_loaded"), 16)
            for name in NAMES:
                def body(it, g):
                    for s in range(2):
                        wait(sp, split_done, g + 2 * s - 2)
                        src = source[name][:, bass.ds(it * 512 + 256 * s, 256)]
                        sp.dma_start(raw[:, s], src.rearrange("(k p) c -> p k c", p=P)).then_inc(w_loaded[s], 16)
                if name == "K":
                    body(1, 4)
                else:
                    with sp.Fori(0, 2) as it:
                        body(it, it * 4 + first(name))

            for n in range(2):
                sp.wait_ge(sem("y_ready"), n + 1)
                sp.dma_start(y_prompt[0, n * P:(n + 1) * P, :], tok[:, n, :]).then_inc(sem("y_stored_sp"), 16)

        @block.gpsimd
        def _(pool):
            steps = [0]

            def link(*instructions):
                for ins in instructions:
                    ins.then_inc(sem("pool_link"), 1)
                steps[0] += len(instructions)
                pool.wait_ge(sem("pool_link"), steps[0])

            with nc.allow_non_contiguous_dma(reason="parameters by channel, a few KB"):
                pool.dma_start(gm1[:, :], g_mem[0].rearrange("(k p) -> p k", p=P)).then_inc(sem("gm_loaded"), 16)
                pool.dma_start(xs_in, x_sample.rearrange("b t d -> (b t) d")).then_inc(sem("start_loaded"), 16)
                pool.dma_start(gn1[:, :], g_norm[0].rearrange("(k p) -> p k", p=P)).then_inc(sem("start_loaded"), 16)
            link(pool.memset(ident[:, :], 0.0), pool.memset(tri[:, :, :], TRI))
            pool.affine_select(out=ident[:, :], in_=ident[:, :], compare_op=ALU.not_equal, fill=1.0, base=0,
                               pattern=[[-1, P]], channel_multiplier=1).then_inc(sem("ident_ready"), 1)
            link(*[pool.affine_select(out=tri[:, a, :], in_=tri[:, a, :], compare_op=ALU.is_ge, fill=0.0, base=0,
                                      pattern=[[1, P]], channel_multiplier=-1) for a in range(2)])
            pool.memset(tri[0:SUB, 0, SUB:P], 0.0).then_inc(sem("tri_ready"), 1)
            with nc.allow_non_contiguous_dma(reason="parameters by channel, a few KB"):
                pool.dma_start(bg1[:, :], b_gate[0].rearrange("(k p) -> p k", p=P)).then_inc(sem("params_loaded"), 16)
                pool.dma_start(gnc[:, :], gn_g[0].rearrange("(k p) -> p k", p=P)).then_inc(sem("params_loaded"), 16)
                pool.dma_start(w00[:, :], w_s[0, :, 0, 0:1].rearrange("h o -> o h").broadcast_to([P, AH])).then_inc(sem("params_loaded"), 16)
                pool.dma_start(gd_raw[:, :, :], win[:, O_GD:O_GD + P].rearrange("(k p) c -> p k c", p=P)).then_inc(sem("params_loaded"), 16)
            pool.wait_ge(sem("memT_done"), KT)
            pool.dma_start(gate[0:RANK, 6, 0:512], w_g_up[0]).then_inc(sem("up_loaded"), 16)
            pool.dma_start(gate[RANK:RANK + 1, 6, 0:512], b_g[0:1, :]).then_inc(sem("up_loaded"), 16)

            for j in range(KT):
                pool.wait_ge(evac_done, j + 1)
                pool.dma_start(scr_kT[:, j, :], stage[:, j % 2, 0:MEM]).then_inc(spilled["K"][j % 2], 16)
            pool.wait_ge(tr_used, KT)
            pool.dma_start(k_prompt[0, 0].rearrange("(n p) h d -> p n (h d)", p=P), tok[:, 0:2, :]).then_inc(sem("kv_stored"), 16)
            pool.wait_ge(tr_used, 2 * KT)
            pool.dma_start(v_prompt[0, 0].rearrange("(n p) h d -> p n (h d)", p=P), tok[:, 2:4, :]).then_inc(sem("kv_stored"), 16)
            pool.wait_ge(tr_used, TR["BV"] + KT)
            pool.dma_start(scr_v, stok[:, :]).then_inc(sem("vs_stored"), 16)
            for j in range(KT):
                pool.wait_ge(evac_done, first("CQ") + j + 1)
                pool.dma_start(scr_qT[:, j, :], stage[:, j % 2, 0:T]).then_inc(spilled["CQ"][j % 2], 16)
            def load_state(b):
                pool.dma_start(s_in[:, b % 4], state_gla[0, b].rearrange("h k v -> k h v")).then_inc(sem(f"ring_loaded{b % 4}"), 16)

            def load_sample_v(b):
                pool.dma_start(v_bc[b % 2], scr_v[b:b + 1, :].broadcast_to([P, D])).then_inc(sem(f"row_loaded{b % 2}"), 16)

            for n in range(NT):
                pool.wait_ge(sem("kv_done"), n + 1)
                load_state(n)
                if n == 2:
                    pool.wait_ge(sem("vs_stored"), 16)
                    for s in range(2):
                        pool.wait_ge(spilled["CQ"][s], 16 * KT // 2)
                    load_sample_v(0)
            pool.wait_ge(sem("state_ready"), NT)
            load_sample_v(1)
            for b in range(B):
                pool.wait_ge(sem("ss_ready"), BH * (b + 1))
                if b + 2 < B:
                    load_sample_v(b + 2)
                pool.dma_start(st_sample[0, b].rearrange("h k v -> k h v"), s_in[:, b % 4]).then_inc(sem(f"ss_stored{b % 4}"), 16)
                if 1 <= b <= 4:
                    pool.wait_ge(sem(f"ss_stored{(b - 1) % 4}"), 16)
                    pool.wait_ge(sem("so_done"), b)
                    load_state(b + 3)
            pool.wait_ge(sem("state_ready"), NT)
            pool.dma_start(st_prompt[0, 0].rearrange("h k v -> k h v"), state[:, :, :]).then_inc(sem("st_stored"), 16)
            pool.wait_ge(sem("dq_ready"), 1)
            pool.dma_start(scr_q, work[0:B, 2048:2048 + D]).then_inc(sem("dq_stored"), 16)
            pool.wait_ge(sem("dq_stored"), 16)
            pool.wait_ge(sem("obs_ready"), 1)
            pool.memset(pz.rearrange("p m b c -> p (m b c)"), 0.0).then_inc(sem("sel_ready"), 1)
            link(pool.memset(sel.rearrange("p h g j -> p (h g j)"), 0.0))
            pool.affine_select(out=sel, in_=sel, compare_op=ALU.not_equal, fill=1.0, base=0,
                               pattern=[[-1, CH], [-4, 2], [-32, 4]], channel_multiplier=1).then_inc(sem("sel_ready"), 1)

            def load_q(b):
                pool.dma_start(q_bc[:, b % 3], scr_q[b:b + 1, :].broadcast_to([P, D])).then_inc(sem(f"row_loaded{b % 3}"), 16)

            for b in range(3):
                load_q(b)
            pool.wait_ge(stage_used, ST["PB"] + KT)
            for i in range(B * MT):
                b = (i + 1) // 2
                if i >= 4:
                    pool.wait_ge(sem("dsc_done"), CH * (i - 3))
                if i % 2 == 1 and 3 <= b < B:
                    load_q(b)
                src = cache_mem_k[0, i // 2].rearrange("(n p) h d -> p n (h d)", p=P)[:, i % 2, :]
                pool.dma_start(kc[:, i % 4], src).then_inc(sem(f"ring_loaded{i % 4}"), 16)
            pool.wait_ge(sem("dsc_done"), CH * B * MT)
            pool.dma_start(lng, ln_v_g[0:1, :].broadcast_to([P, D])).then_inc(sem("a_loaded"), 16)
            pool.dma_start(lnb, ln_v_b[0:1, :].broadcast_to([P, D])).then_inc(sem("a_loaded"), 16)
            pool.dma_start(bs_bc.rearrange("p h t -> p (h t)"), b_s.rearrange("l h t -> l (h t)").broadcast_to([P, D])).then_inc(sem("a_loaded"), 16)
            pool.dma_start(ws_raw, w_s[0].rearrange("h t s -> t h s")).then_inc(sem("ws_loaded"), 16)
            pool.wait_ge(sem("a_loaded"), 48)
            for n in range(NT):
                pool.wait_ge(sem("ln_norm"), n + 1)
                link(pool.tensor_tensor(tok[:, n, :], tok[:, n, :], lng, ALU.mult))
                pool.tensor_tensor(tok[:, n, :], tok[:, n, :], lnb, ALU.add).then_inc(sem("vn_ready"), 1)
            pool.wait_ge(sem("vns_ready"), 1)
            pool.dma_start(vn_sample.rearrange("l b t h c -> (l b t) (h c)"), stok[:, :]).then_inc(sem("vns_stored"), 16)

            def load_v(i):
                g, m, j = i // 8, i // 4 % 2, i % 4
                src = cache_mem_v[0, 4 * g + j].rearrange("(n p) h d -> p n (h d)", p=P)[:, m, :]
                loaded = sem("vc_first_loaded") if i < 2 else sem(f"ring_loaded{(i - 2) % 4}")
                pool.dma_start(v_slots[i], src).then_inc(loaded, 16)

            pool.wait_ge(sem("vn_ready"), NT)
            pool.wait_ge(sem("vns_ready"), 1)
            load_v(0)
            load_v(1)
            pool.wait_ge(sem("mix_done"), AH)
            for i in range(2, B * MT):
                if i >= 6:
                    pool.wait_ge(sem("dpv_done"), i - 3)
                load_v(i)

            pool.wait_ge(sem("mix_lo"), AH)
            for n in range(2):
                pool.wait_ge(spilled["K"][n], 16 * KT // 2)
                pool.wait_ge(spilled["CQ"][n], 16 * KT // 2)
            pool.wait_ge(sem("kv_stored"), 32)
            for h in range(CH):
                if h >= 1:
                    pool.wait_ge(sem("ap_lo"), 3 * h)
                pool.dma_start(q_raw, scr_qT[:, 2 * h:2 * h + 2, :]).then_inc(sem("att_loaded"), 16)
                pool.dma_start(k_raw, scr_kT[:, 2 * h:2 * h + 2, :]).then_inc(sem("att_loaded"), 16)
                pool.dma_start(v_raw, v_prompt[0, 0].rearrange("(n p) h d -> p n h d", p=P)[:, :, h, :]).then_inc(sem("att_loaded"), 16)

            pool.wait_ge(sem("oc_lo"), CH + 1)
            pool.dma_start(x_in, x_prompt[0].rearrange("(n p) d -> p n d", p=P)).then_inc(sem("end_loaded"), 16)
            pool.dma_start(gf_bc, g_final.rearrange("(a d) -> a d", a=1).broadcast_to([P, D])).then_inc(sem("end_loaded"), 16)
            pool.wait_ge(sem("merged"), 2 * KT)
            pool.wait_ge(sem("m_hi"), KT)
            pool.wait_ge(sem("m_lo"), KT)
            pool.dma_start(xs_in, x_sample.rearrange("b t d -> (b t) d")).then_inc(sem("end_loaded"), 16)
            pool.wait_ge(sem("y_ready"), 3)
            pool.dma_start(y_sample.rearrange("b t d -> (b t) d"), stok[:, :]).then_inc(sem("y_stored"), 16)
            pool.wait_ge(sem("kv_stored"), 32)
            pool.wait_ge(sem("kv_stored"), 32)
            pool.wait_ge(sem("st_stored"), 16)
            pool.wait_ge(sem("vns_stored"), 16)
            pool.wait_ge(sem("y_stored"), 16)
            pool.wait_ge(sem("y_stored_sp"), 16 * 2)
            pool.wait_ge(sem("y_stored_act"), 16 * 2)

        @block.scalar
        def _(act):
            A = nc.scalar.activation
            steps = [0]

            def link(*instructions):
                for ins in instructions:
                    ins.then_inc(sem("act_link"), 1)
                steps[0] += len(instructions)
                act.wait_ge(sem("act_link"), steps[0])

            def hi(t, j, pair_loads):
                if isinstance(t, int) and t >= NTILES:
                    return
                act.wait_ge(w_loaded[j // 2], pair_loads)
                wait(act, prod_done, t - 3)
                A(w_hi[:, j], raw[:, j // 2, :, (j % 2) * P:(j % 2 + 1) * P], ACT.Copy).then_inc(hi_ready, 1)

            def square(rows, out, col):
                n = rows.shape[0]
                return A(out, rows, ACT.Square, accum_out=ssq[0:n, col:col + 1])

            act.wait_ge(sem("mem_loaded"), 16)
            act.wait_ge(sem("eps_ready"), 1)
            link(square(mem_in[:, 0, :], junk, 0))
            act.wait_ge(sem("mem_sq"), 1)
            A(rstd[:, 0:MT], ssq[:, 0:MT], ACT.Sqrt, scale=1.0 / D, bias=eps_col[:, :]).then_inc(sem("rt_mem"), 1)
            hi(0, 0, 16)
            hi(1, 1, 16)
            act.wait_ge(sem("gm_loaded"), 16)
            for k in range(KT):
                act.wait_ge(sem("memT_done"), k + 1)
                A(x_hi[:, k, 0:MEM], mem_bank(k), ACT.Copy, scale=gm1[:, k:k + 1]).then_inc(sem("memT_hi"), 1)

            def x_squares(c):
                if c == 0:
                    act.wait_ge(sem("x_loaded"), 16)
                    act.wait_ge(sem("start_loaded"), 32)
                    act.wait_ge(sem("mem_n"), MT)
                link(square(x_in[:, c, :], junk, c))
                if c == NT - 1:
                    link(square(xs_in, junk[0:B, :], NT))
                    A(rstd[:, 0:NT], ssq[:, 0:NT], ACT.Sqrt, scale=1.0 / D, bias=eps_col[:, :]).then_inc(sem("rt_x"), 1)
                    A(rstd[0:B, NT:NT + 1], ssq[0:B, NT:NT + 1], ACT.Sqrt, scale=1.0 / D, bias=eps_col[0:B, :]).then_inc(sem("rt_x"), 1)

            def x_hi_part(k):
                act.wait_ge(sem("xT_done"), k + 1)
                A(h_hi[:, k, 0:T], p67[:, k % 2, :], ACT.Copy, scale=gn1[:, k:k + 1]).then_inc(sem("xT_hi"), 1)

            def evac(name, it, j, g):
                t = g + j
                c = it * 4 + j
                act.wait_ge(prod_done, t + 1)
                src = mm[:, j % 2, :, 0:HALF]
                if name in TR:
                    wait(act, tr_done, c + (TR[name] - 1))
                if name in ST:
                    wait(act, stage_used, c + (ST[name] - 1))
                at_start = isinstance(it, int) and it == 0 and j < 2
                if name == "K" and not at_start:
                    act.wait_ge(spilled["K"][j % 2], 16 * (c // 2))
                if name == "CQ":
                    if at_start:
                        act.wait_ge(tr_done, TR["BV"] + KT)
                    else:
                        act.wait_ge(spilled["CQ"][j % 2], 16 * (c // 2))

                def out3(buf):
                    return buf[:, bass.ds(c, 1), :].rearrange("p o (a b) -> p (o a) b", a=2)

                st = stage[:, j % 2, :].rearrange("p (a b) -> p a b", a=2)
                if name in ("K", "V"):
                    ins = A(stage[:, j % 2, 0:MEM], mm[:, j % 2, 0, 0:MEM], ACT.Copy)
                elif name in ("BV", "PB", "PA", "PC", "OUT"):
                    ins = A(st, src, ACT.Copy)
                elif name == "CQ":
                    A(qsT[:, c, :], mm[:, j % 2, 1, HALF - B:HALF], ACT.Copy).then_inc(sem("qs_ready"), 1)
                    ins = A(st, src, ACT.Copy)
                elif name == "QK":
                    ins = A(out3(t1), src, ACT.Copy)
                elif name == "BZ":
                    ins = A(out3(mz), src, ACT.Silu)
                elif name in ("AZ", "CZ"):
                    ins = A(out3(t1), src, ACT.Silu)
                elif name in ("AV", "AU"):
                    ins = A(st, src, ACT.Gelu_apprx_tanh)
                else:
                    i = "ABC".index(name[1])
                    ins = A(out3(gate), src, ACT.Sigmoid, bias=bg1[:, i * KT + c:i * KT + c + 1])
                ins.then_inc(evac_done, 1)

            def hooks(name, c):
                if name in ("K", "V"):
                    w = KT * BLK[name] + c
                    if w < NT:
                        x_squares(w)
                    elif w < XN + KT:
                        if w >= XN:
                            x_hi_part(w - XN)
                    elif w == XN + KT + 1:
                        act.wait_ge(sem("params_loaded"), 64)
                        A(gd_hi[:, :, :], gd_raw[:, :, :], ACT.Copy).then_inc(sem("gd_hi_ready"), 1)
                    elif w == XN + KT:
                        act.wait_ge(sem("xsT_full"), 1)
                        A(h_hi[:, :, T:TT], hs[:, :, :], ACT.Copy).then_inc(sem("xT_hi"), 1)
                q = KT * (BLK[name] - BLK["BZ"]) + c
                if 4 <= q <= 20:
                    n, step = divmod(q - 4, 4)
                    if step == 0:
                        gla_gate(n)
                    if step == 1 and n < NT:
                        gla_exps(n)
                if name == "GB" and c == 4:
                    gla_out_hi(NT - 1)
                    sample_gates()
                if name == "AZ" and c == 6:
                    act.wait_ge(sem("obs_full"), 2)
                    A(x_hi[:, :, T:TT], mz[:, :, T:TT], ACT.Copy).then_inc(sem("obs_hi"), 1)
                if name == "AU" and c == 2:
                    decode_exp()
                if name == "AU" and 2 <= c <= NT + 2:
                    ln_root(c - 2)
                if name == "OUT" and c >= 2:
                    y_squares(c - 2)
                if name == "GA":
                    act.wait_ge(sem("mix_ready"), c + 1)
                    A(x_hi[:, c, :], t1[:, c, :], ACT.Copy).then_inc(sem("mix_hi"), 1)
                u = KT * (BLK[name] - BLK["CZ"]) + c
                if 0 <= u < 16:
                    h, step = divmod(u, 4)
                    if step == 0:
                        att_exp(h)
                    if step == 3 and h < CH - 1:
                        att_hi(h + 1)
                    if step == 1:
                        att_p(h)
                    if step == 2:
                        att_out(h)
                    if u == KT - 1:
                        act.wait_ge(sem("ocz_ready"), 1)
                        A(x_hi[:, :, T:TT], t1[:, :, T:TT], ACT.Copy).then_inc(sem("oc_hi"), 1)

            def before_evac(name, c):
                q = KT * (BLK[name] - BLK["BZ"]) + c
                if 8 <= q <= 20 and q % 4 == 0:
                    gla_norm(q // 4 - 2)
                if name == "AZ" and c == 6:
                    sample_norm()
                u = KT * (BLK[name] - BLK["CZ"]) + c
                if u == 0:
                    att_hi(0)

            def gla_gate(n):
                if n >= NT:
                    return
                act.wait_ge(sem("z_done"), n + 1)
                link(A(gl, p67[:, 0, :], ACT.Abs))
                link(A(gl, gl, ACT.Exp, scale=-1.0))
                A(gl, gl, ACT.Ln, bias=1.0).then_inc(sem("zln"), 1)

            def gla_exps(n):
                act.wait_ge(sem("cum_done"), n + 1)
                link(A(cols, p67_4[:, :, 63:256:192], ACT.Copy))
                A(eb, p67_4[:, :, 0:P], ACT.Exp).then_inc(sem("exps"), 1)
                A(enb, p67_4[:, :, 0:P], ACT.Exp, scale=-1.0).then_inc(sem("exps"), 1)
                for h in range(BH):
                    ins = A(eBl[:, h, :], p67_4[:, h, P:256], ACT.Exp, scale=-1.0, bias=cols[:, h, 1:2])
                ins.then_inc(sem("exps"), 1)
                for h in range(BH):
                    ins = A(e5[:, h, :], p67_4[:, h, 0:SUB], ACT.Exp, scale=-1.0, bias=cols[:, h, 0:1])
                ins.then_inc(sem("exps"), 1)
                A(e_last, cols[:, :, 1], ACT.Exp)
                A(eB, p67_4[:, :, P:256], ACT.Exp).then_inc(sem("exps"), 1)

            def gla_norm(n):
                if n < 0:
                    return
                if n >= 1:
                    gla_out_hi(n - 1)
                act.wait_ge(sem("o_done"), n + 1)
                for h in range(BH):
                    link(square(p67_4[:, h, :], on[:, h * BV:(h + 1) * BV], h))
                A(rstd[:, 0:BH], ssq[:, 0:BH], ACT.Sqrt, scale=1.0 / BV, bias=eps_col[:, :]).then_inc(sem("o_rt"), 1)
                act.wait_ge(sem("o_rs"), n + 1)
                for h in range(BH):
                    ins = A(on[:, h * BV:(h + 1) * BV], p67_4[:, h, :], ACT.Copy, scale=rden[:, h:h + 1])
                ins.then_inc(sem("on_ready"), 1)

            def gla_out_hi(n):
                act.wait_ge(sem("ob_full"), 2 * (n + 1))
                A(x_hi[:, :, n * P:(n + 1) * P], mz[:, :, n * P:(n + 1) * P], ACT.Copy).then_inc(sem("ob_hi"), 1)

            def sample_gates():
                act.wait_ge(sem("sz_done"), 1)
                link(A(zs, p67[:, 0, 0:BH * B].rearrange("p (h b) -> p h b", b=B), ACT.Abs))
                link(A(zs, zs, ACT.Exp, scale=-1.0))
                A(zs, zs, ACT.Ln, bias=1.0).then_inc(sem("szln"), 1)
                act.wait_ge(sem("szg"), 1)
                A(egs, egs, ACT.Exp, scale=TRI).then_inc(sem("egs_ready"), 1)

            def sample_norm():
                act.wait_ge(sem("so_done"), B)
                link(square(p67[:, 0, 0:BV], ons, 0))
                A(rstd[:, 0:1], ssq[:, 0:1], ACT.Sqrt, scale=1.0 / BV, bias=eps_col[:, :]).then_inc(sem("so_rt"), 1)
                act.wait_ge(sem("so_rs"), 1)
                A(ons, p67[:, 0, 0:BV], ACT.Copy, scale=rden[:, 0:1]).then_inc(sem("ons_ready"), 1)

            def ln_root(n):
                rows = P if n < NT else B
                act.wait_ge(sem("ln_mv"), n + 1)
                A(lstd[0:rows, :], mv[0:rows, 1:2], ACT.Sqrt, bias=eps_col[0:rows, :]).then_inc(sem("ln_rt"), 1)

            def decode_exp():
                act.wait_ge(sem("dmx"), 1)
                A(p32, p67[0:B * CH, 0, 0:MEM], ACT.Exp, scale=C_SCALE, bias=dstat[0:B * CH, 1:2],
                  accum_out=dstat[0:B * CH, 2:3]).then_inc(sem("dexp"), 1)

            def att_hi(h):
                act.wait_ge(prod_done, first("PA") + KT)
                if h == 0:
                    act.wait_ge(sem("dpv_done"), B * MT)
                if h >= 1:
                    act.wait_ge(sem("apv_done"), h)
                act.wait_ge(sem("att_loaded"), 48 * (h + 1))
                A(x_hi[:, 2 * h:2 * h + 2, 0:T], q_raw, ACT.Copy).then_inc(sem("ap_hi"), 1)
                act.wait_ge(sem("att_loaded"), 48 * (h + 1))
                A(k_hi[:, :, :], k_raw, ACT.Copy).then_inc(sem("ap_hi"), 1)
                act.wait_ge(sem("att_loaded"), 48 * (h + 1))
                A(v_hi[:, :, :], v_raw, ACT.Copy).then_inc(sem("ap_hi"), 1)

            def att_exp(h):
                act.wait_ge(sem("anmx"), h + 1)
                if h == 0:
                    act.wait_ge(sem("docs_done"), 1)
                for n in range(NT):
                    A(prob[:, n, :], p45_4[:, n, :], ACT.Exp, scale=C_SCALE, bias=nmx[:, n:n + 1],
                      accum_out=den[:, n:n + 1]).then_inc(sem("aexp"), 1)

            def att_p(h):
                act.wait_ge(sem("apT_done"), h + 1)
                A(pT_hi[:, :, :], p67[:, :, :], ACT.Copy).then_inc(sem("apT_hi"), 1)

            def att_out(h):
                act.wait_ge(sem("oc_full"), h + 1)
                A(x_hi[:, 2 * h:2 * h + 2, 0:T], t1[:, 2 * h:2 * h + 2, 0:T], ACT.Copy).then_inc(sem("oc_hi"), 1)

            def y_squares(c):
                act.wait_ge(tr_used, TR["OUT"] + c + 1)
                act.wait_ge(sem("outs_used"), c + 1)
                wait(act, sem("y_sq"), c)
                for n in range(NT):
                    A(junk2[:, n, :], tok[:, n, c * P:(c + 1) * P], ACT.Square, accum_out=osq[:, n, c:c + 1])
                A(junk2[0:B, NT, :], stok[:, c * P:(c + 1) * P], ACT.Square, accum_out=osq[0:B, NT, c:c + 1]).then_inc(sem("y_sq"), 1)

            for name in NAMES:
                if name == "QK":
                    act.wait_ge(sem("gd_ones"), 1)
                    act.wait_ge(sem("gd_done"), 1)
                    A(gdT[0:RANK, :].rearrange("p (a b) -> p a b", a=2), p67[0:RANK, :, 0:HALF], ACT.Copy).then_inc(sem("gdT_ready"), 1)
                if name == "V":
                    for s in range(2):
                        act.wait_ge(spilled["K"][s], 16 * KT // 2)
                if name == "QK":
                    act.wait_ge(sem("xT_done"), KT + 1)
                if name == "BZ":
                    act.wait_ge(sem("xT_done"), KT + 1)
                if name == "GB":
                    act.wait_ge(sem("params_loaded"), 64)
                if name == "AZ":
                    act.wait_ge(sem("sqk_taken"), 1)
                if name == "PB":
                    act.wait_ge(sem("ss_ready"), BH * (B - 1))
                    for s in range(2):
                        act.wait_ge(spilled["CQ"][s], 16 * KT // 2)
                if name == "AV":
                    act.wait_ge(stage_used, ST["PB"] + KT)
                if name == "AU":
                    act.wait_ge(tr_done, TR["AV"] + KT)
                if name == "GA":
                    act.wait_ge(sem("wsT_ready"), 1)
                    act.wait_ge(sem("dpT_done"), 1)
                if name == "CZ":
                    act.wait_ge(sem("mix_lo"), AH)
                    act.wait_ge(sem("mix_hi"), AH)
                if name == "GC":
                    act.wait_ge(stage_used, ST["PA"] + KT)
                if name == "OUT":
                    act.wait_ge(stage_used, ST["PC"] + KT)

                def body(it, g):
                    for j in range(4):
                        nj = (j + 2) % 4
                        hi(g + j + 2, nj, (it + 2 * BLK[name] + (1 if j < 2 else 2)) * 16)
                        if name in IRREGULAR:
                            before_evac(name, 4 * it + j)
                        evac(name, it, j, g)
                        if name == "PC":
                            c = it * 4 + j
                            act.wait_ge(sem("merged"), c + (KT + 1))
                            A(h_hi[:, bass.ds(c, 1), :], mz[:, bass.ds(c, 1), :], ACT.Copy).then_inc(sem("m_hi"), 1)
                        if name in IRREGULAR:
                            hooks(name, 4 * it + j)
                over_block(act, name, body)

            y_squares(KT - 2)
            y_squares(KT - 1)
            act.wait_ge(sem("y_sums"), 2)
            A(rstd[:, 0:NT], ssq[:, 0:NT], ACT.Sqrt, scale=1.0 / D, bias=eps_col[:, :]).then_inc(sem("y_rt"), 1)
            A(rstd[0:B, NT:NT + 1], ssq[0:B, NT:NT + 1], ACT.Sqrt, scale=1.0 / D, bias=eps_col[0:B, :]).then_inc(sem("y_rt"), 1)
            act.wait_ge(sem("y_rs"), 2)
            act.wait_ge(sem("y_scaled"), KT)
            for n in range(2, NT):
                A(tok[:, n, :], tok[:, n, :], ACT.Copy, scale=rstd[:, n:n + 1]).then_inc(sem("y_ready_act"), 1)
            for n in range(2, NT):
                act.wait_ge(sem("y_ready_act"), n - 1)
                act.dma_start(y_prompt[0, n * P:(n + 1) * P, :], tok[:, n, :]).then_inc(sem("y_stored_act"), 16)

        @block.tensor
        def _(pe):
            MM, TRP = nc.tensor.matmul, nc.tensor.transpose

            def three(out, w, x, first_mm, last_mm):
                MM(out, w[0], x[1], start=first_mm, stop=False)
                MM(out, w[1], x[0], start=False, stop=False)
                return MM(out, w[0], x[0], start=False, stop=last_mm)

            def project(name, j, t):
                pe.wait_ge(split_done, t + 1)
                wait(pe, evac_done, t - 1)
                xh, xl = (x_hi, x_lo) if name in ("K", "V", "PB", "PA", "PC") else (h_hi, h_lo)
                if name in ("K", "V"):
                    spans = [(0, MEM)]
                else:
                    spans = [(0, HALF), (HALF, TT)]
                for k in range(KT):
                    if name == "OUT" and isinstance(t, int) and t == first("OUT"):
                        pe.wait_ge(sem("m_lo"), k + 1)
                    if name == "K" and t == 0:
                        pe.wait_ge(sem("memT_lo"), k + 1)
                    if name == "PA" and t == first("PA"):
                        pe.wait_ge(sem("mix_lo"), k + 1)
                    for wp, xp in ((w_hi, xl), (w_lo, xh), (w_hi, xh)):
                        for a, (c0, c1) in enumerate(spans):
                            ins = MM(mm[:, j % 2, a, 0:c1 - c0], wp[:, j, k, :], xp[:, k, c0:c1],
                                     start=(k == 0 and wp is w_hi and xp is xl), stop=(k == KT - 1 and wp is w_hi and xp is xh))
                ins.then_inc(prod_done, 1)

            def to_tokens(name, it, j, g):
                c = it * 4 + j
                pe.wait_ge(evac_done, g + j + 1)
                wait(pe, tr_used, c + (TR[name] - 1))
                n_rows = MT if name in ("K", "V") else NT
                for n in range(n_rows):
                    ins = TRP(p45[:, j % 2, n * P:(n + 1) * P], stage[:, j % 2, n * P:(n + 1) * P], ident[:, :])
                if n_rows == NT:
                    ins = TRP(p67[0:B, j % 2, 0:P], stage[:, j % 2, T:TT], ident[:, :])
                ins.then_inc(tr_done, 1)

            def hooks(name, c):
                if name in ("K", "V"):
                    w = KT * BLK[name] + c
                    k = w - XN
                    if 0 <= k < KT:
                        pe.wait_ge(sem("x_n"), NT)
                        wait(pe, sem("xT_lo"), k - 1)
                        for n in range(NT):
                            ins = TRP(p67[:, k % 2, n * P:(n + 1) * P], x_in[:, n, k * P:(k + 1) * P], ident[:, :])
                        ins.then_inc(sem("xT_done"), 1)
                    if k == KT:
                        pe.wait_ge(sem("x_n"), NT + 1)
                        pe.wait_ge(sem("xT_lo"), KT)
                        for k in range(KT):
                            ins = TRP(p67[:, 0, k * B:(k + 1) * B], xs_in[:, k * P:(k + 1) * P], ident[0:B, 0:B])
                        ins.then_inc(sem("xT_done"), 1)
                q = KT * (BLK[name] - BLK["BZ"]) + c
                if 4 <= q <= 20:
                    n, step = divmod(q - 4, 4)
                    if step == 0:
                        if n >= 1:
                            gla_turn(n - 1)
                        if n < NT:
                            gla_z(n)
                    elif step == 1:
                        gla_cum(n)
                    elif step == 2:
                        gla_scores(n)
                    else:
                        gla_out(n)
                if name == "GB" and c == 4:
                    for h in range(BH):
                        ins = MM(p67[:, 0, h * B:(h + 1) * B], w_up[:, h * P:(h + 1) * P], gdT[:, T:TT], start=(h == 0), stop=(h == BH - 1), skip_group_check=True)
                    ins.then_inc(sem("sz_done"), 1)
                if name == "GB" and c >= 6:
                    sample_out(c - 6)
                if name == "AZ" and c <= 5:
                    sample_out(c + 2)
                if name == "AZ" and c == 6:
                    pe.wait_ge(sem("ons_ready"), 1)
                    pe.wait_ge(sem("ob_full"), 2 * NT)
                    for a in range(2):
                        ins = TRP(p45[:, 0, a * P:(a + 1) * P], ons[:, a * P:(a + 1) * P], ident[:, :])
                    ins.then_inc(sem("onsT_done"), 1)
                if name == "PB" and c == 0:
                    pe.wait_ge(sem("qs_ready"), KT)
                    for k in range(KT):
                        ins = TRP(p67_8[0:B, k, :], qsT[:, k, :], ident[:, :])
                    ins.then_inc(sem("dq_T"), 1)
                if name == "AU" and c == 6:
                    pe.wait_ge(sem("ws_loaded"), 16)
                    pe.wait_ge(tr_used, TR["AV"] + KT)
                    for h in range(AH):
                        ins = TRP(p45_8[:, h, :], ws_raw[:, h, :], ident[:, :])
                    ins.then_inc(sem("wsT_done"), 1)
                if name == "GA":
                    mix(c)
                if name in ("AU", "PA", "CZ"):
                    decode(name, c)
                u = KT * (BLK[name] - BLK["CZ"]) + c
                if 0 <= u < 16:
                    h, step = divmod(u, 4)
                    if step == 0:
                        att_scores(h)
                    if step == 1:
                        pe.wait_ge(sem("ap_ready"), NT * (h + 1))
                        if h == 0:
                            pe.wait_ge(sem("ocs_ready"), 1)
                        for m in range(MT):
                            for n in range(NT):
                                ins = TRP(p67[:, m, n * P:(n + 1) * P], prob[:, n, m * P:(m + 1) * P], ident[:, :])
                        ins.then_inc(sem("apT_done"), 1)
                    if step == 2:
                        att_pv(h)

            def gla_z(n):
                if n == 0:
                    pe.wait_ge(sem("gdT_ready"), 1)
                    pe.wait_ge(sem("up_loaded"), 32)
                    pe.wait_ge(tr_used, TR["BV"] + KT)
                else:
                    pe.wait_ge(sem("on_ready"), n)
                MM(p67[:, 0, :], gdT[:, n * P:(n + 1) * P], w_up, start=True, stop=True).then_inc(sem("z_done"), 1)

            def gla_cum(n):
                pe.wait_ge(sem("gl_ready"), n + 1)
                pe.wait_ge(sem("tri_ready"), 1)
                for h in range(BH):
                    ins = MM(p67_4[:, h, :], gl[:, h * P:(h + 1) * P], tri[:, :, :], start=True, stop=True)
                ins.then_inc(sem("cum_done"), 1)

            def gla_scores(n):
                pe.wait_ge(sem("ops_ready"), 2 * n + 1)
                if n >= 1:
                    pe.wait_ge(sem("ob_full"), 2 * n)
                for h in range(BH):
                    TRP(p45[:, 0, h * P:(h + 1) * P], eBl[:, h, :], ident[:, :])
                    MM(p45[:, 1, h * P:(h + 1) * P], enb[:, h, :], eb[:, h, :], start=True, stop=True)
                pe.wait_ge(sem("ops_ready"), 2 * n + 2)
                for h in range(BH):
                    ins = MM(p67[0:SUB, 0, h * P:(h + 1) * P], e5[:, h, :], eb[:, h, :], start=True, stop=True)
                ins.then_inc(sem("sc_done"), 1)

            def gla_out(n):
                pe.wait_ge(sem("ssb_ready"), n + 1)
                if n >= 1:
                    pe.wait_ge(sem("state_ready"), n)
                for h in range(BH):
                    v = tok[:, n, h * BV:(h + 1) * BV]
                    if n >= 1:
                        MM(p67_4[:, h, :], eB[:, h, :], state[:, h, :], start=True, stop=False)
                    ins = MM(p67_4[:, h, :], ssb[:, h, :], v, start=(n == 0), stop=True)
                ins.then_inc(sem("o_done"), 1)
                for h in range(BH):
                    ins = MM(p45_4[:, h, :], ktk[:, h, :], tok[:, n, h * BV:(h + 1) * BV], start=True, stop=True)
                ins.then_inc(sem("kv_done"), 1)

            def gla_turn(n):
                pe.wait_ge(sem("on_ready"), n + 1)
                pe.wait_ge(sem("state_ready"), n + 1)
                for v in range(KT):
                    ins = TRP(p45_8[:, v, :], on[:, v * P:(v + 1) * P], ident[:, :])
                ins.then_inc(sem("onT_done"), 1)

            def sample_out(b):
                pe.wait_ge(sem("ss_ready"), BH * (b + 1))
                for h in range(BH):
                    ins = MM(p67[32 * h:32 * h + B, 0, 0:BV], qmask[:, h, b, :], s_in[:, b % 4, h, :],
                             start=(b == 0), stop=(b == B - 1), skip_group_check=True)
                ins.then_inc(sem("so_done"), 1)

            def mix(h):
                if h == 0:
                    pe.wait_ge(sem("vn_ready"), NT)
                    pe.wait_ge(sem("vns_ready"), 1)
                    pe.wait_ge(sem("wsT_ready"), 1)
                if h >= 2:
                    pe.wait_ge(sem("mix_ready"), h - 1)
                for n in range(NT):
                    MM(p45[:, h % 2, n * P:(n + 1) * P], tok[:, n, h * P:(h + 1) * P], wsT[:, h, :], start=True, stop=True)
                TRP(p67[:, h % 2, 0:B], stok[:, h * P:(h + 1) * P], ident[0:B, 0:B]).then_inc(sem("mix_done"), 1)

            def decode(name, c):
                if name == "AU" and c == 2:
                    pe.wait_ge(sem("dsc_done"), B * MT * CH)
                    pe.wait_ge(tr_used, TR["AV"] + KT)
                    pe.wait_ge(sem("stok_in"), 2 * KT)
                    for m in range(MT):
                        ins = TRP(p67[0:B * CH, 0, m * P:(m + 1) * P], sc[:, m, :], ident[:, :])
                    ins.then_inc(sem("dsT_done"), 1)
                if name == "AU" and c == 3:
                    pe.wait_ge(sem("dp_ready"), 1)
                    for m in range(MT):
                        ins = TRP(p67[:, 1, m * B * CH:(m + 1) * B * CH], p32[:, m * P:(m + 1) * P], ident[0:B * CH, 0:B * CH])
                    ins.then_inc(sem("dpT_done"), 1)
                if name == "PA" and c % 2 == 1:
                    r = c // 2
                    g, m = divmod(r, 2)
                    if r == 0:
                        pe.wait_ge(sem("mix_ready"), AH)
                        pe.wait_ge(sem("pm_ready"), 2)
                    for a in range(2):
                        for j in range(4):
                            i = 4 * r + j
                            if a == 0 and i < 2:
                                pe.wait_ge(sem("vc_first_loaded"), 32)
                            elif a == 0:
                                pe.wait_ge(sem(f"ring_loaded{(i - 2) % 4}"), 16 * (ring_keys + (i - 2) // 4 + 1))
                            ins = MM(p45[32 * j:32 * j + 8, a, :], pz[:, m, 4 * g + j, :], v_slots[i][:, a * 512:(a + 1) * 512],
                                     start=(r == 0), stop=(r == 3), skip_group_check=True)
                            if a == 1:
                                ins.then_inc(sem("dpv_done"), 1)
                if name == "CZ" and c == 0:
                    pe.wait_ge(sem("do_ready"), 1)
                    pe.wait_ge(sem("sel_ready"), 2)
                    for k in range(KT):
                        ins = MM(p67[:, 0, k * B:(k + 1) * B], o_sb[:, k * P:(k + 1) * P], sel[:, k // 2, :, :],
                                 start=(k == 0), stop=(k == KT - 1), skip_group_check=True)
                    ins.then_inc(sem("docs_done"), 1)

            def att_scores(h):
                pe.wait_ge(sem("ap_lo"), 3 * (h + 1))
                if h >= 1:
                    pe.wait_ge(sem("oc_full"), h)
                for n in range(NT):
                    for d in range(2):
                        q = [p[:, 2 * h + d, n * P:(n + 1) * P] for p in (x_hi, x_lo)]
                        ins = three(p45_4[:, n, :], q, (k_hi[:, d, :], k_lo[:, d, :]), d == 0, d == 1)
                ins.then_inc(sem("asc_done"), 1)

            def att_pv(h):
                pe.wait_ge(sem("apT_lo"), h + 1)
                for d in range(2):
                    for m in range(MT):
                        v = [p[:, m, d * P:(d + 1) * P] for p in (v_hi, v_lo)]
                        ins = three(p45[:, d, :], v, (pT_hi[:, m, :], pT_lo[:, m, :]), m == 0, m == MT - 1)
                ins.then_inc(sem("apv_done"), 1)

            pe.wait_ge(sem("ident_ready"), 1)
            for k in range(KT):
                pe.wait_ge(sem("mem_n"), MT)
                wait(pe, sem("memT_lo"), k - 3)
                for n in range(MT):
                    ins = TRP(mem_bank(k)[:, n * P:(n + 1) * P], mem_in[:, n, k * P:(k + 1) * P], ident[:, :])
                ins.then_inc(sem("memT_done"), 1)

            for name in NAMES:
                if name == "QK":
                    pe.wait_ge(sem("xT_lo"), KT + 1)
                    pe.wait_ge(sem("gd_split"), 1)
                    for k in range(KT):
                        for wp, xp in ((gd_hi, h_lo), (gd_lo, h_hi), (gd_hi, h_hi)):
                            for a in range(2):
                                ins = MM(p67[:, a, 0:HALF], wp[:, k, :], xp[:, k, a * HALF:(a + 1) * HALF],
                                         start=(k == 0 and xp is h_lo), stop=(k == KT - 1 and wp is gd_hi and xp is h_hi))
                    ins.then_inc(sem("gd_done"), 1)
                if name == "BV":
                    pe.wait_ge(sem("gdT_ready"), 1)
                if name == "PB":
                    pe.wait_ge(sem("obs_ready"), 1)
                if name == "PC":
                    pe.wait_ge(sem("oc_lo"), CH + 1)

                def body(it, g):
                    for j in range(4):
                        project(name, j, g + j)
                        if name in TR and j >= 1:
                            to_tokens(name, it, j - 1, g)
                        if name in IRREGULAR:
                            hooks(name, 4 * it + j)
                    if name in TR:
                        to_tokens(name, it, 3, g)
                over_block(pe, name, body)

        @block.vector
        def _(dve):
            V = nc.vector
            steps = [0]

            def link(ins):
                steps[0] += 1
                ins.then_inc(sem("dve_link"), 1)
                dve.wait_ge(sem("dve_link"), steps[0])

            def f32(x):
                return x.bitcast(F32)

            def lo(t, j):
                if isinstance(t, int) and t >= NTILES:
                    return
                dve.wait_ge(hi_ready, t + 1)
                V.tensor_tensor(w_lo[:, j], raw[:, j // 2, :, (j % 2) * P:(j % 2 + 1) * P], f32(w_hi[:, j]),
                                ALU.subtract).then_inc(split_done, 1)

            def post(name, it, j, g):
                c = it * 4 + j
                cs = bass.ds(c * P, P)
                if name in TR:
                    dve.wait_ge(tr_done, c + (TR[name] + 1))
                    src = p45[:, j % 2, :].rearrange("p (n c) -> p n c", c=P)
                    if name in ("K", "V"):
                        r = 0 if name == "K" else 2
                        V.tensor_copy(tok[:, r:r + 2, cs], src[:, 0:MT, :]).then_inc(tr_used, 1)
                    elif name == "OUT":
                        V.tensor_tensor(stok[:, cs], p67[0:B, j % 2, 0:P], xs_in[:, cs], ALU.add).then_inc(sem("outs_used"), 1)
                        V.tensor_tensor(tok[:, :, cs], src, x_in[:, :, cs], ALU.add).then_inc(tr_used, 1)
                    else:
                        V.tensor_copy(stok[:, cs], p67[0:B, j % 2, 0:P]).then_inc(sem("stok_in"), 1)
                        V.tensor_copy(tok[:, :, cs], src).then_inc(tr_used, 1)
                if name in ST:
                    dve.wait_ge(evac_done, g + j + 1)
                    s = stage[:, j % 2, :]
                    row = bass.ds(c, 1)
                    if name == "AU":
                        V.tensor_tensor(t1[:, c, :], t1[:, c, :], s, ALU.mult).then_inc(stage_used, 1)
                    if name == "PB":
                        V.tensor_tensor(mz[:, c, :], gate[:, c, :], s, ALU.mult).then_inc(stage_used, 1)
                    if name in ("PA", "PC"):
                        g2 = gate[:, row, :].rearrange("p o t -> p (o t)")
                        m2 = mz[:, row, :].rearrange("p o t -> p (o t)")
                        V.tensor_tensor(g2, g2, s, ALU.mult).then_inc(stage_used, 1)
                        dve.wait_ge(stage_used, c + (ST[name] + 1))
                        V.tensor_tensor(m2, m2, g2, ALU.add).then_inc(sem("merged"), 1)
                    if name == "PC":
                        dve.wait_ge(sem("m_hi"), c + 1)
                        V.tensor_tensor(h_lo[:, row, :], mz[:, row, :], f32(h_hi[:, row, :]), ALU.subtract).then_inc(sem("m_lo"), 1)

            def hooks(name, c):
                if name in ("K", "V"):
                    w = KT * BLK[name] + c
                    k = w - XN
                    if w == NT - 1:
                        dve.wait_ge(sem("rt_x"), 2)
                        link(V.reciprocal(rstd[:, 0:NT], rstd[:, 0:NT]))
                        link(V.reciprocal(rstd[0:B, NT:NT + 1], rstd[0:B, NT:NT + 1]))
                        for n in range(NT):
                            V.tensor_scalar(x_in[:, n, :], x_in[:, n, :], rstd[:, n:n + 1], None, ALU.mult).then_inc(sem("x_n"), 1)
                        V.tensor_scalar(xs_in, xs_in, rstd[0:B, NT:NT + 1], None, ALU.mult).then_inc(sem("x_n"), 1)
                    elif 0 <= k < KT:
                        dve.wait_ge(sem("xT_hi"), k + 1)
                        V.scalar_tensor_tensor(out=h_lo[:, k, 0:T], in0=p67[:, k % 2, :], scalar=gn1[:, k:k + 1],
                                               in1=f32(h_hi[:, k, 0:T]), op0=ALU.mult, op1=ALU.subtract).then_inc(sem("xT_lo"), 1)
                    elif k == KT + 1:
                        dve.wait_ge(sem("gd_hi_ready"), 1)
                        V.tensor_tensor(gd_lo[:, :, :], gd_raw[:, :, :], f32(gd_hi[:, :, :]), ALU.subtract).then_inc(sem("gd_split"), 1)
                    elif k == KT:
                        dve.wait_ge(sem("xT_done"), KT + 1)
                        V.tensor_tensor(hs[:, :, :], p67[:, 0, 0:KT * B].rearrange("p (k b) -> p k b", b=B),
                                        gn1[:, :].unsqueeze(2).broadcast_to([P, KT, B]), ALU.mult).then_inc(sem("xsT_full"), 1)
                        dve.wait_ge(sem("xT_hi"), KT + 1)
                        V.tensor_tensor(h_lo[:, :, T:TT], hs[:, :, :], f32(h_hi[:, :, T:TT]), ALU.subtract).then_inc(sem("xT_lo"), 1)
                q = KT * (BLK[name] - BLK["BZ"]) + c
                if 4 <= q <= 20:
                    n, step = divmod(q - 4, 4)
                    if step == 0:
                        if n >= 1:
                            dve.wait_ge(sem("o_rt"), n)
                            V.reciprocal(rden[:, 0:BH], rstd[:, 0:BH]).then_inc(sem("o_rs"), 1)
                            if n >= 2:
                                gla_out_lo(n - 2)
                            gla_full(n - 1)
                        if n < NT:
                            gla_gates(n)
                    elif step == 1:
                        gla_ops(n)
                    elif step == 2:
                        gla_masks(n)
                    else:
                        gla_state(n)
                if name == "GB" and c == 4:
                    gla_out_lo(NT - 1)
                    sample_prepare()
                if name == "GB" and c >= 5:
                    sample_state(c - 5)
                if name == "AZ" and c <= 4:
                    sample_state(c + 3)
                if name == "AZ" and c == 6:
                    dve.wait_ge(sem("so_rt"), 1)
                    V.reciprocal(rden[:, 0:1], rstd[:, 0:1]).then_inc(sem("so_rs"), 1)
                    dve.wait_ge(sem("onsT_done"), 1)
                    for a in range(2):
                        m = mz[:, a:KT:2, T:TT]
                        o = p45[:, 0, a * P:(a + 1) * P].rearrange("p (h c) -> p h c", c=32)[:, :, 0:B]
                        V.scalar_tensor_tensor(out=m, in0=o, scalar=gnc[:, a:a + 1], in1=m,
                                               op0=ALU.mult, op1=ALU.mult).then_inc(sem("obs_full"), 1)
                    dve.wait_ge(sem("obs_hi"), 1)
                    V.tensor_tensor(x_lo[:, :, T:TT], mz[:, :, T:TT], f32(x_hi[:, :, T:TT]), ALU.subtract).then_inc(sem("obs_ready"), 1)
                if name == "PB" and c == 1:
                    dve.wait_ge(sem("dq_T"), 1)
                    V.tensor_copy(work[0:B, 2048:2048 + D].rearrange("p (a b) -> p a b", a=2), p67[0:B, :, :]).then_inc(sem("dq_ready"), 1)
                if name == "AV" and c >= 1:
                    decode_scores(range(max(0, 2 * c - 3), 2 * c - 1))
                if name == "AU":
                    if c == 6:
                        dve.wait_ge(sem("wsT_done"), 1)
                        dve.wait_ge(sem("st_stored"), 16)
                        V.scalar_tensor_tensor(out=wsT, in0=p45_8, scalar=1.0 / TRI, in1=tri[:, 1:2, :].broadcast_to([P, AH, P]),
                                               op0=ALU.mult, op1=ALU.mult).then_inc(sem("wsT_ready"), 1)
                    if c == 0:
                        decode_scores((13, 14))
                    if c == 1:
                        decode_scores((15,))
                    if c == 2:
                        decode_softmax()
                    if c == 3:
                        dve.wait_ge(sem("dpT_done"), 1)
                        dve.wait_ge(sem("sel_ready"), 1)
                        pT = p67[:, 1, 0:MT * B * CH].rearrange("p (m b h) -> p m b h", b=B, h=CH)
                        for g in range(2):
                            V.tensor_copy(pz[:, :, 4 * g:4 * g + 4, 4 * g:4 * g + 4], pT[:, :, 4 * g:4 * g + 4, :]).then_inc(sem("pm_ready"), 1)
                    if 2 <= c <= NT + 2:
                        layer_norm(c - 2)
                if name == "GA":
                    mix(c)
                if name == "OUT" and c >= 2:
                    y_scale(c - 2)
                if name == "PA" and c == 7:
                    dve.wait_ge(sem("dpv_done"), B * MT)
                    V.tensor_copy(o_sb.rearrange("p (a b) -> p a b", a=2), p45[:, :, :]).then_inc(sem("do_ready"), 1)
                if name == "CZ" and c == 0:
                    att_lo(0)
                    dve.wait_ge(sem("docs_done"), 1)
                    V.tensor_copy(ocs[:, :, :], p67[:, 0, 0:KT * B].rearrange("p (k b) -> p k b", b=B)).then_inc(sem("ocs_ready"), 1)
                u = KT * (BLK[name] - BLK["CZ"]) + c
                if 0 <= u < 16:
                    h, step = divmod(u, 4)
                    if step == 0:
                        att_soft(h)
                    if step == 3 and h < CH - 1:
                        att_lo(h + 1)
                    if step == 1:
                        dve.wait_ge(sem("apT_hi"), h + 1)
                        V.tensor_tensor(pT_lo[:, :, :], p67[:, :, :], f32(pT_hi[:, :, :]), ALU.subtract).then_inc(sem("apT_lo"), 1)
                    if step == 2:
                        dve.wait_ge(sem("apv_done"), h + 1)
                        dve.wait_ge(evac_done, first("CZ") + 2 * h + 2)
                        tc = t1[:, 2 * h:2 * h + 2, 0:T]
                        V.tensor_tensor(tc, p45[:, :, :], tc, ALU.mult).then_inc(sem("oc_full"), 1)
                        n_hi = h + 1 if h < 2 else h + 2
                        dve.wait_ge(sem("oc_hi"), n_hi)
                        V.tensor_tensor(x_lo[:, 2 * h:2 * h + 2, 0:T], tc, f32(x_hi[:, 2 * h:2 * h + 2, 0:T]), ALU.subtract).then_inc(sem("oc_lo"), 1)
                    if u == KT - 1:
                        dve.wait_ge(evac_done, first("CZ") + KT)
                        V.tensor_tensor(t1[:, :, T:TT], t1[:, :, T:TT], ocs[:, :, :], ALU.mult).then_inc(sem("ocz_ready"), 1)
                        dve.wait_ge(sem("oc_hi"), 3)
                        V.tensor_tensor(x_lo[:, :, T:TT], t1[:, :, T:TT], f32(x_hi[:, :, T:TT]), ALU.subtract).then_inc(sem("oc_lo"), 1)

            def gla_gates(n):
                dve.wait_ge(sem("zln"), n + 1)
                V.scalar_tensor_tensor(out=gl, in0=p67[:, 0, :], scalar=0.0, in1=gl, op0=ALU.min,
                                       op1=ALU.subtract).then_inc(sem("gl_ready"), 1)

            def gla_ops(n):
                q = t1[:, 0:BH, n * P:(n + 1) * P]
                k = t1[:, BH:2 * BH, n * P:(n + 1) * P]
                dve.wait_ge(sem("exps"), 5 * n + 1)
                dve.wait_ge(evac_done, first("QK") + KT)
                V.scalar_tensor_tensor(out=eb, in0=q, scalar=Q_SCALE, in1=eb, op0=ALU.mult, op1=ALU.mult)
                dve.wait_ge(sem("exps"), 5 * n + 2)
                V.tensor_tensor(enb, k, enb, ALU.mult)
                dve.wait_ge(sem("exps"), 5 * n + 3)
                V.tensor_tensor(eBl, k, eBl, ALU.mult)
                dve.wait_ge(sem("exps"), 5 * n + 4)
                V.tensor_tensor(e5, k[:, :, 0:SUB], e5, ALU.mult).then_inc(sem("ops_ready"), 1)
                dve.wait_ge(sem("exps"), 5 * n + 5)
                V.scalar_tensor_tensor(out=eB, in0=q, scalar=Q_SCALE, in1=eB, op0=ALU.mult, op1=ALU.mult).then_inc(sem("ops_ready"), 1)

            def gla_masks(n):
                dve.wait_ge(sem("sc_done"), n + 1)
                V.tensor_copy(ktk, p45[:, 0, :].rearrange("p (h c) -> p h c", c=P))
                link(V.scalar_tensor_tensor(out=ssb, in0=p45[:, 1, :].rearrange("p (h c) -> p h c", c=P), scalar=1.0 / TRI,
                                            in1=tri[:, 0:1, :].broadcast_to([P, BH, P]), op0=ALU.mult, op1=ALU.mult))
                V.tensor_copy(ssb[0:SUB, :, SUB:P], p67[0:SUB, 0, :].rearrange("p (h c) -> p h c", c=P)[:, :, SUB:P]).then_inc(sem("ssb_ready"), 1)

            def gla_state(n):
                dve.wait_ge(sem("kv_done"), n + 1)
                if n == 0:
                    V.tensor_copy(state[:, :, :], p45_4).then_inc(sem("state_ready"), 1)
                else:
                    for h in range(BH):
                        ins = V.scalar_tensor_tensor(out=state[:, h, :], in0=state[:, h, :], scalar=e_last[:, h:h + 1],
                                                     in1=p45_4[:, h, :], op0=ALU.mult, op1=ALU.add)
                    ins.then_inc(sem("state_ready"), 1)

            def gla_full(n):
                dve.wait_ge(sem("onT_done"), n + 1)
                if n == 0:
                    dve.wait_ge(sem("params_loaded"), 64)
                    dve.wait_ge(evac_done, first("BZ") + KT)
                for a in range(2):
                    m = mz[:, a:KT:2, n * P:(n + 1) * P]
                    V.scalar_tensor_tensor(out=m, in0=p45_8[:, a:KT:2, :], scalar=gnc[:, a:a + 1], in1=m,
                                           op0=ALU.mult, op1=ALU.mult).then_inc(sem("ob_full"), 1)

            def gla_out_lo(n):
                dve.wait_ge(sem("ob_hi"), n + 1)
                s = slice(n * P, (n + 1) * P)
                V.tensor_tensor(x_lo[:, :, s], mz[:, :, s], f32(x_hi[:, :, s]), ALU.subtract)

            def sample_prepare():
                dve.wait_ge(sem("sz_done"), 1)
                link(V.memset(qmask.rearrange("p h b c -> p (h b c)"), 0.0))
                V.tensor_scalar(qmask.rearrange("p h b c -> p h (b c)")[:, :, 0:B * B:B + 1], t1[:, 0:BH, T:TT], Q_SCALE, None,
                                ALU.mult)
                V.tensor_copy(ksT[:, :, :], t1[:, BH:2 * BH, T:TT]).then_inc(sem("sqk_taken"), 1)
                dve.wait_ge(sem("szln"), 1)
                V.scalar_tensor_tensor(out=egs, in0=p67[:, 0, 0:BH * B].rearrange("p (h b) -> p h b", b=B), scalar=0.0,
                                       in1=zs, op0=ALU.min, op1=ALU.subtract).then_inc(sem("szg"), 1)

            def sample_state(b):
                s = b % 4
                dve.wait_ge(sem(f"row_loaded{b % 2}"), 16 * (b // 2 + 1))
                if b == 0:
                    dve.wait_ge(sem("egs_ready"), 1)
                    dve.wait_ge(sem("sqk_taken"), 1)
                else:
                    dve.wait_ge(sem("ss_ready"), BH * b)
                for h in range(BH):
                    V.tensor_scalar(tmp_kv[:, h, :], v_bc[b % 2][:, h * BV:(h + 1) * BV], ksT[:, h, b:b + 1], None, ALU.mult).then_inc(sem("tmp_kv"), 1)
                dve.wait_ge(sem(f"ring_loaded{s}"), 16 * (b // 4 + 1))
                for h in range(BH):
                    dve.wait_ge(sem("tmp_kv"), BH * b + h + 1)
                    V.scalar_tensor_tensor(out=s_in[:, s, h, :], in0=s_in[:, s, h, :], scalar=egs[:, h, b:b + 1],
                                           in1=tmp_kv[:, h, :], op0=ALU.mult, op1=ALU.add).then_inc(sem("ss_ready"), 1)

            def layer_norm(n):
                rows, r = (tok[:, n, :], P) if n < NT else (stok[:, :], B)
                if n == 0:
                    dve.wait_ge(tr_used, TR["AV"] + KT)
                    dve.wait_ge(sem("stok_in"), 2 * KT)
                for a in range(2):
                    link(V.bn_stats(stats[0:r, a, :], rows[:, a * 512:(a + 1) * 512]))
                V.bn_aggr(mv[0:r, :], stats[0:r, :, :]).then_inc(sem("ln_mv"), 1)
                dve.wait_ge(sem("ln_rt"), n + 1)
                link(V.reciprocal(lrst[0:r, :], lstd[0:r, :]))
                V.tensor_scalar(rows, rows, mv[0:r, 0:1], lrst[0:r, :], ALU.subtract, ALU.mult).then_inc(sem("ln_norm"), 1)
                if n == NT:
                    dve.wait_ge(sem("ln_norm"), NT + 1)
                    dve.wait_ge(sem("a_loaded"), 48)
                    link(V.tensor_tensor(rows, rows, lng[0:B, :], ALU.mult))
                    V.tensor_tensor(rows, rows, lnb[0:B, :], ALU.add).then_inc(sem("vns_ready"), 1)

            def mix(h):
                dve.wait_ge(sem("mix_done"), h + 1)
                if h == 0:
                    dve.wait_ge(sem("a_loaded"), 48)
                    dve.wait_ge(sem("params_loaded"), 64)
                V.tensor_tensor(mtmp[:, 0:T].rearrange("p (n t) -> p n t", t=P), p45[:, h % 2, :].rearrange("p (n t) -> p n t", t=P),
                                bs_bc[:, h:h + 1, :].broadcast_to([P, NT, P]), ALU.add)
                link(V.tensor_scalar(mtmp[:, T:TT], p67[:, h % 2, 0:B], w00[:, h:h + 1], bs_bc[:, h, 0:1], ALU.mult, ALU.add))
                V.tensor_tensor(t1[:, h, :], t1[:, h, :], mtmp, ALU.mult).then_inc(sem("mix_ready"), 1)
                dve.wait_ge(sem("mix_hi"), h + 1)
                V.tensor_tensor(x_lo[:, h, :], t1[:, h, :], f32(x_hi[:, h, :]), ALU.subtract).then_inc(sem("mix_lo"), 1)

            def decode_scores(tiles):
                for i in tiles:
                    b, m = divmod(i, MT)
                    dve.wait_ge(sem(f"ring_loaded{i % 4}"), 16 * (ring_states + i // 4 + 1))
                    if m == 0:
                        dve.wait_ge(sem(f"row_loaded{b % 3}"), 16 * (row_v[b % 3] + b // 3 + 1))
                    for h in range(CH):
                        k = kc[:, i % 4, h * CD:(h + 1) * CD]
                        V.tensor_tensor_reduce(k, k, q_bc[:, b % 3, h * CD:(h + 1) * CD], 1.0, 0.0, ALU.mult, ALU.add,
                                               sc[:, m, b * CH + h:b * CH + h + 1]).then_inc(sem("dsc_done"), 1)

            def decode_softmax():
                n = B * CH
                dve.wait_ge(sem("dsT_done"), 1)
                link(V.tensor_reduce(dstat[0:n, 0:1], p67[0:n, 0, 0:MEM], AX_X, ALU.max))
                V.tensor_scalar(dstat[0:n, 1:2], dstat[0:n, 0:1], -C_SCALE, None, ALU.mult).then_inc(sem("dmx"), 1)
                dve.wait_ge(sem("dexp"), 1)
                link(V.reciprocal(dstat[0:n, 3:4], dstat[0:n, 2:3]))
                V.tensor_scalar(p32, p32, dstat[0:n, 3:4], None, ALU.mult).then_inc(sem("dp_ready"), 1)

            def att_lo(h):
                for n, (dst, src, top) in enumerate(((x_lo[:, 2 * h:2 * h + 2, 0:T], q_raw, x_hi[:, 2 * h:2 * h + 2, 0:T]),
                                                     (k_lo[:, :, :], k_raw, k_hi[:, :, :]), (v_lo[:, :, :], v_raw, v_hi[:, :, :]))):
                    dve.wait_ge(sem("ap_hi"), 3 * h + n + 1)
                    V.tensor_tensor(dst, src, f32(top), ALU.subtract).then_inc(sem("ap_lo"), 1)

            def att_soft(h):
                dve.wait_ge(sem("asc_done"), h + 1)
                link(V.tensor_reduce(mx, p45_4, AX_X, ALU.max))
                V.tensor_scalar(nmx, mx, -C_SCALE, None, ALU.mult).then_inc(sem("anmx"), 1)
                dve.wait_ge(sem("aexp"), NT * (h + 1))
                link(V.reciprocal(rden, den))
                for n in range(NT):
                    V.tensor_scalar(prob[:, n, :], prob[:, n, :], rden[:, n:n + 1], None, ALU.mult).then_inc(sem("ap_ready"), 1)

            def y_scale(c):
                dve.wait_ge(sem("y_sq"), c + 1)
                cs = slice(c * P, (c + 1) * P)
                V.tensor_tensor(tok[:, :, cs], tok[:, :, cs], gf_bc[:, cs].unsqueeze(1).broadcast_to([P, NT, P]), ALU.mult)
                V.tensor_tensor(stok[:, cs], stok[:, cs], gf_bc[0:B, cs], ALU.mult).then_inc(sem("y_scaled"), 1)

            V.memset(eps_col, EPS).then_inc(sem("eps_ready"), 1)
            V.memset(gdT, 1.0).then_inc(sem("gd_ones"), 1)
            dve.wait_ge(sem("mem_loaded"), 16)
            V.tensor_tensor_reduce(mz_flat[:, 2 * D:3 * D], mem_in[:, 1, :], mem_in[:, 1, :], 1.0, 0.0, ALU.mult, ALU.add,
                                   ssq[:, 1:2]).then_inc(sem("mem_sq"), 1)
            dve.wait_ge(sem("rt_mem"), 1)
            link(V.reciprocal(rstd[:, 0:MT], rstd[:, 0:MT]))
            for n in range(MT):
                V.tensor_scalar(mem_in[:, n, :], mem_in[:, n, :], rstd[:, n:n + 1], None, ALU.mult).then_inc(sem("mem_n"), 1)
            lo(0, 0)
            lo(1, 1)
            dve.wait_ge(sem("gm_loaded"), 16)
            for k in range(KT):
                dve.wait_ge(sem("memT_hi"), k + 1)
                V.scalar_tensor_tensor(out=x_lo[:, k, 0:MEM], in0=mem_bank(k), scalar=gm1[:, k:k + 1],
                                       in1=f32(x_hi[:, k, 0:MEM]), op0=ALU.mult, op1=ALU.subtract).then_inc(sem("memT_lo"), 1)
            dve.wait_ge(sem("start_loaded"), 32)

            for name in NAMES:
                if name == "BV":
                    dve.wait_ge(sem("kv_stored"), 32)
                    dve.wait_ge(sem("kv_stored"), 32)
                if name == "AV":
                    for s in range(4):
                        dve.wait_ge(sem(f"ss_stored{s}"), 16 * B // 4)
                if name == "OUT":
                    dve.wait_ge(sem("end_loaded"), 48)
                    dve.wait_ge(sem("end_loaded"), 48)
                    dve.wait_ge(sem("vns_stored"), 16)

                def body(it, g):
                    for j in range(4):
                        lo(g + j + 2, (j + 2) % 4)
                        post(name, it, j, g)
                        if name in IRREGULAR:
                            hooks(name, 4 * it + j)
                over_block(dve, name, body)

            y_scale(KT - 2)
            dve.wait_ge(sem("y_sq"), KT)
            V.tensor_reduce(ssq[:, 0:NT], osq[:, 0:NT, :], AX_X, ALU.add).then_inc(sem("y_sums"), 1)
            V.tensor_reduce(ssq[0:B, NT:NT + 1], osq[0:B, NT:NT + 1, :], AX_X, ALU.add).then_inc(sem("y_sums"), 1)
            y_scale(KT - 1)
            dve.wait_ge(sem("y_rt"), 2)
            V.reciprocal(rstd[:, 0:NT], rstd[:, 0:NT]).then_inc(sem("y_rs"), 1)
            V.reciprocal(rstd[0:B, NT:NT + 1], rstd[0:B, NT:NT + 1]).then_inc(sem("y_rs"), 1)
            dve.wait_ge(sem("y_rs"), 2)
            dve.wait_ge(sem("y_scaled"), KT)
            for n in range(2):
                V.tensor_scalar(tok[:, n, :], tok[:, n, :], rstd[:, n:n + 1], None, ALU.mult).then_inc(sem("y_ready"), 1)
            V.tensor_scalar(stok[:, :], stok[:, :], rstd[0:B, NT:NT + 1], None, ALU.mult).then_inc(sem("y_ready"), 1)


_INS = ['x_prompt', 'x_sample', 'state_gla', 'cache_mem_k', 'cache_mem_v', 'mem_prompt', 'g_norm', 'w_in',
        'b_gate', 'w_s', 'b_s', 'ln_v_g', 'ln_v_b', 'w_g_up', 'b_g', 'gn_g', 'g_mem', 'w_mem_kv', 'w_branch',
        'w_out', 'g_final']
_OUTS = [((1, 512, 1024), 'float32'), ((8, 1, 1024), 'float32'), ((1, 1, 4, 128, 256), 'float32'),
         ((1, 1, 256, 4, 256), 'float32'), ((1, 1, 256, 4, 256), 'float32'), ((1, 8, 4, 128, 256), 'float32'),
         ((1, 8, 1, 8, 128), 'float32')]


def kernel(**inputs):
    import numpy as _np
    import concourse.bacc as _bacc
    from concourse import mybir as _mybir
    from concourse.bass_utils import run_bass_kernel_spmd as _run

    nc = _bacc.Bacc("TRN2", target_bir_lowering=False, num_devices=1)
    arrays, args = {}, []
    for name in _INS:
        a = _np.ascontiguousarray(inputs[name])
        arrays[f"in_{name}_dram"] = a
        args.append(nc.dram_tensor(f"in_{name}_dram", a.shape, _mybir.dt.from_np(a.dtype), kind="ExternalInput").ap())
    for i, (shape, dtype) in enumerate(_OUTS):
        dt = _mybir.dt.from_np(_np.dtype(dtype))
        args.append(nc.dram_tensor(f"out_{i}_dram", shape, dt, kind="ExternalOutput").ap())
    bass_gated_parallel_step(nc, *args)
    r = _run(nc, [arrays], core_ids=[0])
    return tuple(r.results[0][f"out_{i}_dram"] for i in range(len(_OUTS)))
```
